# Optimizing a Trainium2 kernel written in Bass

```python
import jax
import jax.numpy as jnp
from jax import lax
import numpy as np
import math
import jax, jax.numpy as jnp

D_MODEL = 1024
BATCH = 1
SEQ = 512
DEPTH = 2

GLA_HEADS = 4
GLA_DK = 64
GLA_DV = 128
GLA_GATE_RANK = 16
GLA_GATE_TEMP = 16.0
GLA_CHUNK = 64
NSA_HEADS = 8
NSA_KV_GROUPS = 2
NSA_HPG = NSA_HEADS // NSA_KV_GROUPS
NSA_DH = 64
NSA_CMP_BLOCK = 32
NSA_CMP_STRIDE = 16
NSA_CMP_HIDDEN = 128
NSA_SEL_BLOCK = 64
NSA_TOPN = 16
NSA_WINDOW = 512
NSA_QBLOCK = 128
NSA_BRANCHES = 3
SGU_WIDTH = 2 * D_MODEL
SGU_GROUPS = 8
SGU_CHUNK = 128
FFN_HIDDEN = 4 * D_MODEL
NORM_EPS = 1e-6
NEG_BIG = -1e30
POS_BIG = 1e30

EVEN_PROJ_SIZES = (GLA_HEADS * GLA_DK, GLA_HEADS * GLA_DK, GLA_HEADS * GLA_DV, GLA_GATE_RANK, GLA_HEADS * GLA_DV, NSA_HEADS * NSA_DH, NSA_KV_GROUPS * NSA_DH, NSA_KV_GROUPS * NSA_DH, NSA_KV_GROUPS * NSA_DH, NSA_KV_GROUPS * NSA_DH, NSA_KV_GROUPS * NSA_DH, NSA_KV_GROUPS * NSA_DH, NSA_HEADS * NSA_BRANCHES)
EVEN_PROJ_WIDTH = sum(EVEN_PROJ_SIZES)
EVEN_MIX_WIDTH = GLA_HEADS * GLA_DV + NSA_HEADS * NSA_DH


def _rms_norm(x, g):
    xf = x.astype(jnp.float32)
    y = xf * lax.rsqrt(jnp.mean(xf * xf, axis=-1, keepdims=True) + NORM_EPS)
    return (y * g).astype(x.dtype)

def _masked_softmax(s, mask):
    m = mask.astype(jnp.float32)
    s = jnp.where(mask, s, NEG_BIG)
    p = jnp.exp(s - jnp.max(s, axis=-1, keepdims=True)) * m
    return p / jnp.maximum(jnp.sum(p, axis=-1, keepdims=True), 1e-30)

def _squared_relu_mlp(x, w1, w2):
    h = jax.nn.relu(x @ w1)
    return (h * h) @ w2

def _gla(q, k, v, g_lr, r, w_gate, b_gate, norm_g):
    f32 = jnp.float32
    bsz, seq, _ = q.shape
    c = GLA_CHUNK
    nc = seq // c
    glog = jax.nn.log_sigmoid((g_lr @ w_gate + b_gate).astype(f32)) / GLA_GATE_TEMP

    def chunks(t, d):
        return t.astype(f32).reshape(bsz, nc, c, GLA_HEADS, d).transpose(0, 3, 1, 2, 4)

    qc = chunks(q, GLA_DK) * (GLA_DK ** -0.5)
    kc = chunks(k, GLA_DK)
    vc = chunks(v, GLA_DV)
    b = jnp.cumsum(chunks(glog, GLA_DK), axis=3)
    b_last = b[:, :, :, -1:, :]
    q_t = qc * jnp.exp(b)
    k_t = kc * jnp.exp(-b)
    k_end = kc * jnp.exp(b_last - b)
    causal = jnp.tril(jnp.ones((c, c), dtype=bool))
    a = jnp.where(causal, jnp.einsum('bhnid,bhnjd->bhnij', q_t, k_t), 0.0)
    o_intra = jnp.einsum('bhnij,bhnjv->bhniv', a, vc)
    ds = jnp.einsum('bhnjd,bhnjv->bhndv', k_end, vc)
    decay = jnp.exp(b_last[:, :, :, 0, :])

    def step(state, inp):
        dec, d = inp
        return dec[..., None] * state + d, state

    s0 = jnp.zeros((bsz, GLA_HEADS, GLA_DK, GLA_DV), f32)
    _, s_prev = lax.scan(step, s0, (jnp.moveaxis(decay, 2, 0), jnp.moveaxis(ds, 2, 0)))
    s_prev = jnp.moveaxis(s_prev, 0, 2)
    o = o_intra + jnp.einsum('bhnid,bhndv->bhniv', q_t, s_prev)
    o = o.transpose(0, 2, 3, 1, 4).reshape(bsz, seq, GLA_HEADS, GLA_DV)
    o = o * lax.rsqrt(jnp.mean(o * o, axis=-1, keepdims=True) + NORM_EPS) * norm_g
    o = o.reshape(bsz, seq, GLA_HEADS * GLA_DV) * jax.nn.silu(r.astype(f32))
    return o.astype(q.dtype)

def _nsa(q, kc, vc, ks, vs, kw, vw, gate_logits, cmp_pos, cmp_w1, cmp_w2):
    f32 = jnp.float32
    bsz, seq, _ = q.shape
    g_n, hpg, dh, qb_len, w = NSA_KV_GROUPS, NSA_HPG, NSA_DH, NSA_QBLOCK, NSA_WINDOW
    n_qb = seq // qb_len
    n_cmp = (seq - NSA_CMP_BLOCK) // NSA_CMP_STRIDE + 1
    n_sel = seq // NSA_SEL_BLOCK
    topn = min(NSA_TOPN, n_sel)
    scale = dh ** -0.5

    def kv_heads(t):
        return t.reshape(bsz, seq, g_n, dh)

    cmp_idx = jnp.arange(n_cmp)[:, None] * NSA_CMP_STRIDE + jnp.arange(NSA_CMP_BLOCK)[None, :]

    def compress(t, i):
        blocks = kv_heads(t)[:, cmp_idx] + cmp_pos[i][None, None, :, None, :]
        blocks = blocks.transpose(0, 3, 1, 2, 4).reshape(bsz, g_n, n_cmp, NSA_CMP_BLOCK * dh)
        return jax.nn.gelu(blocks @ cmp_w1[i]) @ cmp_w2[i]

    k_cmp = compress(kc, 0)
    v_cmp = compress(vc, 1)
    cmp_start = jnp.arange(n_cmp) * NSA_CMP_STRIDE
    cmp_end = cmp_start + NSA_CMP_BLOCK - 1
    sel_start = jnp.arange(n_sel) * NSA_SEL_BLOCK
    overlap = ((cmp_start[:, None] < sel_start[None, :] + NSA_SEL_BLOCK)
               & (cmp_start[:, None] + NSA_CMP_BLOCK > sel_start[None, :])).astype(f32)

    k_sel = kv_heads(ks).reshape(bsz, n_sel, NSA_SEL_BLOCK, g_n, dh).transpose(0, 3, 1, 2, 4)
    v_sel = kv_heads(vs).reshape(bsz, n_sel, NSA_SEL_BLOCK, g_n, dh).transpose(0, 3, 1, 2, 4)
    pad = ((0, 0), (0, 0), (w, 0), (0, 0))
    k_win = jnp.pad(kv_heads(kw).transpose(0, 2, 1, 3), pad)
    v_win = jnp.pad(kv_heads(vw).transpose(0, 2, 1, 3), pad)

    qb = (q * scale).reshape(bsz, n_qb, qb_len, g_n, hpg, dh).transpose(1, 0, 3, 4, 2, 5)
    gb = jax.nn.sigmoid(gate_logits.astype(f32)).reshape(bsz, n_qb, qb_len, g_n, hpg, NSA_BRANCHES)
    gb = gb.transpose(1, 0, 3, 4, 2, 5)
    b_ix = jnp.arange(bsz)[:, None, None, None]
    g_ix = jnp.arange(g_n)[None, :, None, None]
    within = jnp.arange(NSA_SEL_BLOCK)
    win_off = jnp.arange(qb_len + w)
    sel_j = jnp.arange(n_sel)

    def block(args):
        n, qn, gn = args
        t = n * qb_len + jnp.arange(qb_len)
        s_c = jnp.einsum('bghqd,bgcd->bghqc', qn, k_cmp).astype(f32)
        p_c = _masked_softmax(s_c, cmp_end[None, :] <= t[:, None])
        o_c = jnp.einsum('bghqc,bgcd->bghqd', p_c.astype(v_cmp.dtype), v_cmp)
        imp = jnp.einsum('bgqc,cj->bgqj', jnp.sum(p_c, axis=2), overlap)
        cur = t // NSA_SEL_BLOCK
        forced = (sel_j[None, :] == 0) | (sel_j[None, :] == cur[:, None]) | (sel_j[None, :] == cur[:, None] - 1)
        allowed = sel_start[None, :] <= t[:, None]
        score = jnp.where(forced, POS_BIG, jnp.where(allowed, imp, NEG_BIG))
        top_val, top_idx = lax.top_k(score, topn)
        blk_ok = top_val > 0.5 * NEG_BIG
        k_g = k_sel[b_ix, g_ix, top_idx]
        v_g = v_sel[b_ix, g_ix, top_idx]
        kpos = top_idx[..., None] * NSA_SEL_BLOCK + within
        ok = blk_ok[..., None] & (kpos <= t[None, None, :, None, None])
        s_s = jnp.einsum('bghqd,bgqnkd->bghqnk', qn, k_g).astype(f32)
        s_s = s_s.reshape(bsz, g_n, hpg, qb_len, topn * NSA_SEL_BLOCK)
        p_s = _masked_softmax(s_s, ok.reshape(bsz, g_n, 1, qb_len, topn * NSA_SEL_BLOCK))
        p_s = p_s.reshape(bsz, g_n, hpg, qb_len, topn, NSA_SEL_BLOCK).astype(v_g.dtype)
        o_s = jnp.einsum('bghqnk,bgqnkd->bghqd', p_s, v_g)
        k_w = lax.dynamic_slice_in_dim(k_win, n * qb_len, qb_len + w, axis=2)
        v_w = lax.dynamic_slice_in_dim(v_win, n * qb_len, qb_len + w, axis=2)
        kpos_w = n * qb_len - w + win_off
        ok_w = (kpos_w[None, :] >= 0) & (kpos_w[None, :] <= t[:, None]) & (kpos_w[None, :] > t[:, None] - w)
        s_w = jnp.einsum('bghqd,bgkd->bghqk', qn, k_w).astype(f32)
        p_w = _masked_softmax(s_w, ok_w)
        o_w = jnp.einsum('bghqk,bgkd->bghqd', p_w.astype(v_w.dtype), v_w)
        out = gn[..., 0:1] * o_c + gn[..., 1:2] * o_s + gn[..., 2:3] * o_w
        return out.astype(q.dtype)

    o = lax.map(block, (jnp.arange(n_qb), qb, gb))
    return o.transpose(1, 0, 4, 2, 3, 5).reshape(bsz, seq, NSA_HEADS * dh)

def _even_mixer(x, w_in, w_out, gla_w_gate, gla_b_gate, gla_norm, nsa_gate_b, nsa_cmp_pos, nsa_cmp_w1, nsa_cmp_w2):
    offsets = [int(o) for o in np.cumsum(EVEN_PROJ_SIZES)[:-1]]
    gq, gk, gv, glr, gr, nq, kc, vc, ks, vs, kw, vw, ng = jnp.split(x @ w_in, offsets, axis=-1)
    o_a = _gla(gq, gk, gv, glr, gr, gla_w_gate, gla_b_gate, gla_norm)
    o_b = _nsa(nq, kc, vc, ks, vs, kw, vw, ng + nsa_gate_b, nsa_cmp_pos, nsa_cmp_w1, nsa_cmp_w2)
    return jnp.concatenate([o_a, o_b], axis=-1) @ w_out

def _sgu_mixer(x, w_in, ln_g, ln_b, w_s, b_s, w_out):
    bsz, seq, _ = x.shape
    h = jax.nn.gelu(x @ w_in)
    u, v = jnp.split(h, 2, axis=-1)
    vf = v.astype(jnp.float32)
    mu = jnp.mean(vf, axis=-1, keepdims=True)
    var = jnp.mean((vf - mu) ** 2, axis=-1, keepdims=True)
    v = ((vf - mu) * lax.rsqrt(var + NORM_EPS) * ln_g + ln_b).astype(x.dtype)
    n_ch = seq // SGU_CHUNK
    v = v.reshape(bsz, n_ch, SGU_CHUNK, SGU_GROUPS, SGU_WIDTH // SGU_GROUPS)
    w_causal = jnp.where(jnp.tril(jnp.ones((SGU_CHUNK, SGU_CHUNK), dtype=bool)), w_s, 0.0)
    mixed = jnp.einsum('gts,bnsgc->bntgc', w_causal, v) + b_s.T[:, :, None]
    y = u * mixed.reshape(bsz, seq, SGU_WIDTH)
    return y @ w_out

def first_inputs(seed: int = 0) -> dict:
    key = jax.random.key(seed)
    k = jax.random.split(key, 20)
    ne = (DEPTH + 1) // 2
    no = DEPTH // 2
    f32 = jnp.float32

    def normal(kk, shape):
        return jax.random.normal(kk, shape, f32)

    def dense(kk, shape, fan_in):
        return normal(kk, shape) * (fan_in ** -0.5)

    return {
        'x': normal(k[0], (BATCH, SEQ, D_MODEL)),
        'norm_g': 1.0 + 0.05 * normal(k[1], (DEPTH, 4, D_MODEL)),
        'ffn_w1': dense(k[2], (DEPTH, D_MODEL, FFN_HIDDEN), D_MODEL),
        'ffn_w2': dense(k[3], (DEPTH, FFN_HIDDEN, D_MODEL), FFN_HIDDEN),
        'e_w_in': dense(k[4], (ne, D_MODEL, EVEN_PROJ_WIDTH), D_MODEL),
        'e_w_out': dense(k[5], (ne, EVEN_MIX_WIDTH, D_MODEL), EVEN_MIX_WIDTH),
        'gla_w_gate': dense(k[6], (ne, GLA_GATE_RANK, GLA_HEADS * GLA_DK), GLA_GATE_RANK),
        'gla_b_gate': 0.1 * normal(k[7], (ne, GLA_HEADS * GLA_DK)),
        'gla_norm': 1.0 + 0.05 * normal(k[8], (ne, GLA_HEADS, GLA_DV)),
        'nsa_gate_b': 0.1 * normal(k[9], (ne, NSA_HEADS * NSA_BRANCHES)),
        'nsa_cmp_pos': 0.1 * normal(k[10], (ne, 2, NSA_CMP_BLOCK, NSA_DH)),
        'nsa_cmp_w1': dense(k[11], (ne, 2, NSA_CMP_BLOCK * NSA_DH, NSA_CMP_HIDDEN), NSA_CMP_BLOCK * NSA_DH),
        'nsa_cmp_w2': dense(k[12], (ne, 2, NSA_CMP_HIDDEN, NSA_DH), NSA_CMP_HIDDEN),
        'o_w_in': dense(k[13], (no, D_MODEL, 2 * SGU_WIDTH), D_MODEL),
        'o_ln_g': 1.0 + 0.05 * normal(k[14], (no, SGU_WIDTH)),
        'o_ln_b': 0.02 * normal(k[15], (no, SGU_WIDTH)),
        'o_w_s': dense(k[16], (no, SGU_GROUPS, SGU_CHUNK, SGU_CHUNK), SGU_CHUNK),
        'o_b_s': 1.0 + 0.1 * normal(k[17], (no, SGU_GROUPS, SGU_CHUNK)),
        'o_w_out': dense(k[18], (no, SGU_WIDTH, D_MODEL), SGU_WIDTH),
    }

def first_block(x, norm_g, ffn_w1, ffn_w2, e_w_in, e_w_out, gla_w_gate, gla_b_gate, gla_norm, nsa_gate_b, nsa_cmp_pos, nsa_cmp_w1, nsa_cmp_w2, o_w_in, o_ln_g, o_ln_b, o_w_s, o_b_s, o_w_out):
    h = x
    for layer in range(DEPTH):
        i = layer // 2
        xn = _rms_norm(h, norm_g[layer, 0])
        if layer % 2 == 0:
            m = _even_mixer(xn, e_w_in[i], e_w_out[i], gla_w_gate[i], gla_b_gate[i], gla_norm[i],
                            nsa_gate_b[i], nsa_cmp_pos[i], nsa_cmp_w1[i], nsa_cmp_w2[i])
        else:
            m = _sgu_mixer(xn, o_w_in[i], o_ln_g[i], o_ln_b[i], o_w_s[i], o_b_s[i], o_w_out[i])
        h = h + _rms_norm(m, norm_g[layer, 1])
        f = _squared_relu_mlp(_rms_norm(h, norm_g[layer, 2]), ffn_w1[layer], ffn_w2[layer])
        h = h + _rms_norm(f, norm_g[layer, 3])
    return h


DEPTH_2 = 1

HEAD_DIM = 64
DIL_GROUPS = ((128, 1), (512, 4), (2048, 16))
HEADS_PER_GROUP = 4
N_GROUPS = len(DIL_GROUPS)
N_HEADS_A = HEADS_PER_GROUP * N_GROUPS
N_HEADS_B = 4
WIDTH_A = N_HEADS_A * HEAD_DIM
WIDTH_A_OUT = HEADS_PER_GROUP * HEAD_DIM
WIDTH_B = N_HEADS_B * HEAD_DIM
N_BRANCH = 2
SPLIT_SIZES = (WIDTH_A, WIDTH_A, WIDTH_A, WIDTH_B, WIDTH_B, WIDTH_B, N_HEADS_B, D_MODEL, D_MODEL)
SPLIT_POINTS = tuple(int(v) for v in np.cumsum(SPLIT_SIZES)[:-1])
D_IN = int(sum(SPLIT_SIZES))
D_FF = -(-8 * D_MODEL // (3 * 256)) * 256
BLOCK = 128
ALIBI_MAX = 8.0
EPS = 1e-6
N_MOD = 6


def rms_norm(x, g):
    xf = x.astype(jnp.float32)
    y = xf * lax.rsqrt(jnp.mean(xf * xf, axis=-1, keepdims=True) + EPS)
    return (y * g.astype(jnp.float32)).astype(x.dtype)

def alibi_slopes():
    h = np.arange(1, N_HEADS_A + 1, dtype=np.float32)
    return jnp.asarray(2.0 ** (-ALIBI_MAX * h / N_HEADS_A), dtype=jnp.float32)

def dilated_group_attention(q, k, v, window, dilation, slopes):
    B, S, H, Dh = q.shape
    L = S // dilation
    nb = -(-L // BLOCK)
    Lp = nb * BLOCK
    pad_end = Lp - L

    def split(t):
        return t.reshape(B, L, dilation, H, Dh).transpose(0, 2, 1, 3, 4)

    def band(t):
        t = jnp.pad(split(t), ((0, 0), (0, 0), (BLOCK, pad_end), (0, 0), (0, 0)))
        t = t.reshape(B, dilation, nb + 1, BLOCK, H, Dh)
        return jnp.concatenate([t[:, :, :-1], t[:, :, 1:]], axis=3)

    qb = jnp.pad(split(q), ((0, 0), (0, 0), (0, pad_end), (0, 0), (0, 0)))
    qb = qb.reshape(B, dilation, nb, BLOCK, H, Dh)
    kb, vb = band(k), band(v)

    scores = jnp.einsum('brnqhd,brnkhd->brnhqk', qb, kb).astype(jnp.float32) * (Dh ** -0.5)
    qi = jnp.arange(BLOCK)[:, None]
    kj = jnp.arange(2 * BLOCK)[None, :]
    dist = qi + BLOCK - kj
    kpos = jnp.arange(nb)[:, None, None] * BLOCK + kj[None] - BLOCK
    valid = (dist >= 0) & (dist <= window // dilation) & (kpos >= 0)
    bias = -slopes[:, None, None] * (dist * dilation).astype(jnp.float32)[None]
    logits = jnp.where(valid[None, None, :, None], scores + bias, -jnp.inf)
    lse = jax.nn.logsumexp(logits, axis=-1)
    p = jnp.exp(logits - lse[..., None])
    out = jnp.einsum('brnhqk,brnkhd->brnqhd', p.astype(v.dtype), vb)
    out = out.reshape(B, dilation, Lp, H, Dh)[:, :, :L].transpose(0, 2, 1, 3, 4).reshape(B, S, H, Dh)
    lse = lse.transpose(0, 1, 2, 4, 3).reshape(B, dilation, Lp, H)[:, :, :L]
    lse = lse.transpose(0, 2, 1, 3).reshape(B, S, H)
    return out, lse

def dilated_mixture(qa, ka, va):
    B, S, _ = qa.shape
    shp = (B, S, N_HEADS_A, HEAD_DIM)
    qa, ka, va = qa.reshape(shp), ka.reshape(shp), va.reshape(shp)
    slopes = alibi_slopes()
    outs, lses = [], []
    for g, (w, d) in enumerate(DIL_GROUPS):
        sl = slice(g * HEADS_PER_GROUP, (g + 1) * HEADS_PER_GROUP)
        o, l = dilated_group_attention(qa[:, :, sl], ka[:, :, sl], va[:, :, sl], w, d, slopes[sl])
        outs.append(o)
        lses.append(l)
    outs = jnp.stack(outs, axis=0)
    alpha = jax.nn.softmax(jnp.stack(lses, axis=0), axis=0)
    y = jnp.sum(alpha[..., None].astype(outs.dtype) * outs, axis=0)
    return y.reshape(B, S, WIDTH_A_OUT)

def forgetting_attention(qb, kb, vb, f_logit, b_forget):
    B, S, _ = qb.shape
    H, Dh = N_HEADS_B, HEAD_DIM
    q = qb.reshape(B, S, H, Dh)
    k = kb.reshape(B, S, H, Dh)
    v = vb.reshape(B, S, H, Dh)
    log_f = jax.nn.log_sigmoid(f_logit.astype(jnp.float32) + b_forget.astype(jnp.float32))
    F = jnp.cumsum(log_f, axis=1).transpose(0, 2, 1)
    nb = S // BLOCK
    q_blocks = q.reshape(B, nb, BLOCK, H, Dh).transpose(1, 0, 2, 3, 4)
    F_blocks = F.reshape(B, H, nb, BLOCK).transpose(2, 0, 1, 3)
    kpos = jnp.arange(S)
    scale = Dh ** -0.5

    def one_block(args):
        i, qi, Fi = args
        s = jnp.einsum('bqhd,bkhd->bhqk', qi, k).astype(jnp.float32) * scale
        s = s + (Fi[..., :, None] - F[..., None, :])
        qpos = i * BLOCK + jnp.arange(BLOCK)
        s = jnp.where(kpos[None, :] <= qpos[:, None], s, -jnp.inf)
        p = jax.nn.softmax(s, axis=-1)
        return jnp.einsum('bhqk,bkhd->bqhd', p.astype(v.dtype), v)

    out = lax.map(one_block, (jnp.arange(nb), q_blocks, F_blocks))
    return out.transpose(1, 0, 2, 3, 4).reshape(B, S, H * Dh)

def token_mixer(h, w_in, b_forget, w_up_a, w_up_b, w_out):
    z = h @ w_in
    qa, ka, va, qb, kb, vb, fz, gza, gzb = jnp.split(z, SPLIT_POINTS, axis=-1)
    ya = dilated_mixture(qa, ka, va) @ w_up_a
    yb = forgetting_attention(qb, kb, vb, fz, b_forget) @ w_up_b
    merged = jax.nn.sigmoid(gza) * ya + jax.nn.sigmoid(gzb) * yb
    return merged @ w_out

def swiglu(h, w_ffn_in, w_ffn_out):
    gate, up = jnp.split(h @ w_ffn_in, 2, axis=-1)
    return (jax.nn.silu(gate) * up) @ w_ffn_out

def second_inputs(seed: int = 0) -> dict:
    key = jax.random.key(seed)
    ks = jax.random.split(key, 16)
    f32 = jnp.float32
    nrm = lambda k, shape, s: jax.random.normal(k, shape, f32) * s
    x = jax.random.normal(ks[0], (BATCH, SEQ, D_MODEL), f32)
    c = jax.random.normal(ks[1], (BATCH, D_MODEL), f32)
    w_ada = nrm(ks[2], (DEPTH_2, D_MODEL, N_MOD * D_MODEL), 0.5 * D_MODEL ** -0.5)
    b_ada = nrm(ks[3], (DEPTH_2, N_MOD * D_MODEL), 0.02)
    norm_mix = 1.0 + nrm(ks[4], (DEPTH_2, D_MODEL), 0.02)
    w_in = nrm(ks[5], (DEPTH_2, D_MODEL, D_IN), D_MODEL ** -0.5)
    b_forget = jnp.linspace(1.0, 5.0, N_HEADS_B, dtype=f32)[None] + nrm(ks[6], (DEPTH_2, N_HEADS_B), 0.1)
    w_up_a = nrm(ks[7], (DEPTH_2, WIDTH_A_OUT, D_MODEL), WIDTH_A_OUT ** -0.5)
    w_up_b = nrm(ks[8], (DEPTH_2, WIDTH_B, D_MODEL), WIDTH_B ** -0.5)
    w_out = nrm(ks[9], (DEPTH_2, D_MODEL, D_MODEL), D_MODEL ** -0.5)
    norm_ffn = 1.0 + nrm(ks[10], (DEPTH_2, D_MODEL), 0.02)
    w_ffn_in = nrm(ks[11], (DEPTH_2, D_MODEL, 2 * D_FF), D_MODEL ** -0.5)
    w_ffn_out = nrm(ks[12], (DEPTH_2, D_FF, D_MODEL), D_FF ** -0.5)
    norm_final = 1.0 + nrm(ks[13], (D_MODEL,), 0.02)
    return {"x": x, "c": c, "w_ada": w_ada, "b_ada": b_ada, "norm_mix": norm_mix,
            "w_in": w_in, "b_forget": b_forget, "w_up_a": w_up_a, "w_up_b": w_up_b,
            "w_out": w_out, "norm_ffn": norm_ffn, "w_ffn_in": w_ffn_in,
            "w_ffn_out": w_ffn_out, "norm_final": norm_final}

def second_block(x, c, w_ada, b_ada, norm_mix, w_in, b_forget, w_up_a, w_up_b, w_out,
              norm_ffn, w_ffn_in, w_ffn_out, norm_final):
    c_act = jax.nn.silu(c)
    for l in range(DEPTH_2):
        mod = c_act @ w_ada[l] + b_ada[l]
        sh1, sc1, g1, sh2, sc2, g2 = [m[:, None, :] for m in jnp.split(mod, N_MOD, axis=-1)]
        h = rms_norm(x, norm_mix[l]) * (1.0 + sc1) + sh1
        x = x + g1 * token_mixer(h, w_in[l], b_forget[l], w_up_a[l], w_up_b[l], w_out[l])
        h = rms_norm(x, norm_ffn[l]) * (1.0 + sc2) + sh2
        x = x + g2 * swiglu(h, w_ffn_in[l], w_ffn_out[l])
    return rms_norm(x, norm_final)


def setup_inputs(seed=0):
    out = dict(first_inputs(seed))
    for name, value in second_inputs(seed + 1).items():
        if name != "x":
            out[name + "_2"] = value
    return out


def reference(
    x, norm_g, ffn_w1, ffn_w2, e_w_in, e_w_out, gla_w_gate, gla_b_gate, gla_norm, nsa_gate_b,
    nsa_cmp_pos, nsa_cmp_w1, nsa_cmp_w2, o_w_in, o_ln_g, o_ln_b, o_w_s, o_b_s, o_w_out, c_2,
    w_ada_2, b_ada_2, norm_mix_2, w_in_2, b_forget_2, w_up_a_2, w_up_b_2, w_out_2, norm_ffn_2,
    w_ffn_in_2, w_ffn_out_2, norm_final_2,
):
    x = first_block(
        x, norm_g, ffn_w1, ffn_w2, e_w_in, e_w_out, gla_w_gate, gla_b_gate, gla_norm,
        nsa_gate_b, nsa_cmp_pos, nsa_cmp_w1, nsa_cmp_w2, o_w_in, o_ln_g, o_ln_b, o_w_s, o_b_s,
        o_w_out,
    )
    return second_block(
        x, c_2, w_ada_2, b_ada_2, norm_mix_2, w_in_2, b_forget_2, w_up_a_2, w_up_b_2, w_out_2,
        norm_ffn_2, w_ffn_in_2, w_ffn_out_2, norm_final_2,
    )


_drawn_inputs = setup_inputs


def setup_inputs(seed=0):
    import zlib

    import numpy as np

    out = dict(_drawn_inputs(seed))
    spreads = {}
    factors = {'nsa_gate_b': 4.701,
     'o_ln_g': 3.8,
     'o_ln_b': 8.0,
     'b_ada_2': 6.216,
     'norm_mix_2': 8.0,
     'norm_ffn_2': 8.0,
     'norm_final_2': 2.781}
    for name, (base, spread) in spreads.items():
        noise = np.random.default_rng([zlib.crc32(name.encode()), seed]).standard_normal(out[name].shape)
        drawn = base * np.exp(spread * noise) if base else spread * noise
        out[name] = jnp.asarray(drawn.astype(out[name].dtype))
    for name, factor in factors.items():
        out[name] = (out[name] * factor).astype(out[name].dtype)
    return out
```

```python
from contextlib import ExitStack

import numpy as np
import concourse.bass as bass
from concourse import mybir

F32 = mybir.dt.float32
F32R = mybir.dt.float32r
I32 = mybir.dt.int32
ALU = mybir.AluOpType
ACT = mybir.ActivationFunctionType
AX = mybir.AxisListType

P = 128
SEQ, D = 512, 1024
NT = SEQ // P
DK = D // P
EPS = 1e-6
NEG = -1e30
TILE = 2048
HD = 64

GQ, GK, GV, GLR, GR, NQ, KC = 0, 256, 512, 1024, 1040, 1552, 2064
KS, VS, KW, VW, NG = 2320, 2448, 2576, 2704, 2832
GLA_HEADS, CH = 4, 64
RANK = 16
NG_COLS = 24
CMP_N, CMP_STRIDE, CMP_BLOCK = 31, 16, 32
FFN = 4096
SGU = 2048
QA, KA, VA, QB, KB, VB, FZ, GZA, GZB = 0, 768, 1536, 2304, 2560, 2816, 3072, 3076, 4100
DILATED = ((128, 1), (512, 4), (2048, 16))
SLOTS = 4
DFF = 2816
ALIBI = [float(np.float32(2.0 ** (-8.0 * i / 12))) for i in range(1, 13)]


class Chain:

    def __init__(self, engine, semaphore):
        self.engine, self.semaphore, self.n = engine, semaphore, 0

    def link(self, instruction):
        instruction.then_inc(self.semaphore, 1)
        self.n = self.n + 1
        self.engine.wait_ge(self.semaphore, self.n)

    def enter(self, it, links):
        self.base, self.links = self.n, links
        self.n = it * links + self.base

    def leave(self, turns):
        self.n = self.base + turns * self.links


class Stage:

    def __init__(self, first, count, unit, done, per):
        self.first, self.count, self.unit, self.done, self.per = first, count, unit, done, per


def plan():
    order = [("e_cols", 8, 2), ("e_small", 1, 2), ("e_v", 3, 2), ("e_out", 4, 0),
             ("f0_up0", 6, 2), ("f0_down0", 6, 0), ("f0_up1", 6, 2), ("f0_down1", 6, 0),
             ("f0_up2", 4, 2), ("f0_down2", 4, 0),
             ("o_u", 8, 2), ("o_v", 8, 2), ("o_out", 8, 0),
             ("f1_up0", 6, 2), ("f1_down0", 6, 0), ("f1_up1", 6, 2), ("f1_down1", 6, 0),
             ("f1_up2", 4, 2), ("f1_down2", 4, 0),
             ("s_qk", 8, 2), ("s_v", 4, 2), ("s_small", 1, 1), ("s_upa", 1, 8), ("s_upb", 1, 8),
             ("s_ga", 4, 2), ("s_gb", 4, 2), ("s_out", 4, 0),
             ("g_up0", 12, 2), ("g_down0", 6, 0), ("g_up1", 10, 2), ("g_down1", 5, 0)]
    stages, n, u, done = {}, 0, 0, 0
    for name, count, units in order:
        stages[name] = Stage(n, count, u, done, units or 1)
        n += count
        u += count * units
        done += count * units if units else count + 3
    return stages, n, u


def program(nc, A, out):
    S, N_TILES, N_UNITS = plan()
    TWO_PIECES = (S["e_cols"].first + 7, S["e_v"].first + 2, S["e_small"].first)
    ctx = ExitStack()

    def loaded(n):
        return 16 * (n // 2 + 1) + 16 * sum(t <= n and t % 2 == n % 2 for t in TWO_PIECES)

    def tiles(eng, stage, body):
        pairs = stage.count // 2
        if pairs > 1:
            with eng.Fori(0, pairs) as it:
                body(it * 2, 0, it)
                body(it * 2 + 1, 1, it)
        elif pairs:
            body(0, 0, 0)
            body(1, 1, 0)
        if stage.count % 2:
            body(stage.count - 1, 0, pairs)

    with ctx:
        def sb(name, shape, dt=F32):
            return ctx.enter_context(nc.sbuf_tensor(name, shape, dt))

        KB_ = 256
        h = sb("h", [P, NT, D])
        w_raw = sb("w_raw", [P, 2, TILE])
        w_hi = sb("w_hi", [P, 2, TILE], F32R)
        w_lo = sb("w_lo", [P, 2, TILE], F32R)
        g1_row = sb("g1_row", [P, D])
        g2_row = sb("g2_row", [P, D])
        ident = sb("ident", [P, P])
        ones = sb("ones", [P, P])
        causal = sb("causal", [P, P])
        col_gain = sb("col_gain", [P, 6, DK])
        col_bias = sb("col_bias", [P, 2, DK])
        col_mod = sb("col_mod", [P, 4, DK])
        b_ada_col = sb("b_ada_col", [P, 48])
        c_col = sb("c_col", [P, DK])
        small = sb("small", [P, 64])
        ss = sb("ss", [P, 16])
        rstd = sb("rstd", [P, 16])
        neg_half = sb("neg_half", [P, 1])
        att_stat = sb("att_stat", [P, 2, 16])
        chunk_decay = sb("chunk_decay", [P, 2, 8])
        branch_gate = sb("branch_gate", [P, NT, NG_COLS])
        gla_norm = sb("gla_norm", [P, GLA_HEADS])
        b_gate = sb("b_gate", [P, 2])
        ln_g_col = sb("ln_g_col", [P, 16])
        ln_b_col = sb("ln_b_col", [P, 16])
        b_forget = sb("b_forget", [4, 1])
        f_row = sb("f_row", [P, SEQ])

        arena = [0]

        def place(name, shape, at_kb, dt=F32):
            stack = ExitStack()
            if at_kb:
                arena[0] += 1
                stack.enter_context(nc.sbuf_tensor(f"pad{arena[0]}", [P, int(at_kb * KB_)], F32))
            t = stack.enter_context(nc.sbuf_tensor(name, shape, dt))
            stack.close()
            return t

        W_, M_, R_, E_, X_, Y_ = 0, 4, 20, 24, 34, 66
        work = place("work", [P, 2, SEQ], W_)
        m = place("m", [P, NT, D], M_)
        row_gain = place("row_gain", [P, D], R_)
        x_hi = place("x_hi", [P, DK, SEQ], X_, F32R)
        x_lo = place("x_lo", [P, DK, SEQ], X_ + 16, F32R)
        h2_hi = place("h2_hi", [P, 12, SEQ], Y_, F32R)
        h2_lo = place("h2_lo", [P, 12, SEQ], Y_ + 24, F32R)
        ada_w = place("ada_w", [P, 2, 1024], Y_ + 48)
        ada_acc = place("ada_acc", [P, 1024], Y_ + 56)
        e_t = place("e_t", [P, 12, SEQ], Y_)
        k_s = place("k_s", [P, 2, SEQ], Y_ + 24)
        k_w = place("k_w", [P, 2, SEQ], Y_ + 28)
        x_c = place("x_c", [P, 4, SEQ], Y_ + 32)
        o_gla = place("o_gla", [P, 4, SEQ], Y_ + 32)
        g_v = place("g_v", [P, NT, 512], Y_ + 40)
        v_sw = place("v_sw", [P, NT, 256], Y_ + 48)
        cmp_x = place("cmp_x", [P, 2, 8, 2, CMP_N], W_)
        k_end = place("k_end", [P, 2, SEQ], Y_ + 52)
        am = place("am", [P, 2, 2, P], Y_ + 56)
        k_end_t = place("k_end_t", [P, 2, P], Y_ + 58)
        gla_mask = place("gla_mask", [P, P], Y_ + 59)
        keep = place("keep", [P, SEQ], Y_ + 60)
        cmp_hid = place("cmp_hid", [P, 4, 32], Y_ + 62)
        k_cmp = place("k_cmp", [P, 2, 32], Y_ + 62.5)
        v_cmp = place("v_cmp", [P, 2, HD], Y_ + 62.75)
        cmp_add = place("cmp_add", [P, NT, 32], Y_ + 63.25)
        cmp_w1 = [place("cmp_w1_k", [P, 16, P], E_), place("cmp_w1_v", [P, 16, P], M_ + 8)]
        cmp_one = place("cmp_one", [P, NT, 32], Y_ + 59.5)
        cum = place("cum", [P, 2, SEQ], M_)
        t1 = place("t1", [P, 2, SEQ], M_ + 4)
        state = place("state", [P, 2, 8, P], M_ + 8)
        state_flat = place("state_flat", [P, 2, SEQ], M_ + 8)
        gn_inv = place("gn_inv", [P, 2, SEQ], M_ + 12)
        w_gate = place("w_gate", [P, 256], R_)
        gate_rows = place("gate_rows", [P, NG_COLS], R_ + 1)
        cmp_pos = place("cmp_pos", [P, 2, 16], R_ + 1.25)
        cmp_w2 = place("cmp_w2", [P, 2, HD], R_ + 1.5)
        mix_hi = place("mix_hi", [P, DK, SEQ], X_, F32R)
        mix_lo = place("mix_lo", [P, DK, SEQ], X_ + 16, F32R)
        prob = place("prob", [P, 2, 1280], E_)
        prob_n = place("prob_n", [P, 2, 1152], E_)
        prob_t = place("prob_t", [P, 2, SEQ], R_)
        u_t = place("u_t", [P, 16, SEQ], Y_)
        v_ln = place("v_ln", [P, NT, SGU], Y_ + 32)
        y_hi = place("y_hi", [P, 16, SEQ], Y_, F32R)
        y_lo = place("y_lo", [P, 16, SEQ], X_, F32R)
        w_s = place("w_s", [P, 8, P], E_)
        w_sum = place("w_sum", [P, 8, P], E_)
        w_st = place("w_st", [P, 8, P], E_ + 4)
        bn = place("bn", [P, 4, 6], E_ + 8)
        mv = place("mv", [P, NT, 2], E_ + 8.25)
        b_s_row = place("b_s_row", [P, 8, P], R_)
        small_row = place("small_row", [P, P], E_ + 8.5)
        q_k = place("q_k", [P, 16, SEQ], Y_)
        v_ab = place("v_ab", [P, NT, 1024], M_)
        bias_near = place("bias_near", [P, SLOTS, 256], W_)
        bias_far = place("bias_far", [P, 2, SLOTS, SEQ], Y_ + 32)
        yt_hi = place("yt_hi", [P, 4, SEQ], Y_ + 48, F32R)
        yt_lo = place("yt_lo", [P, 4, SEQ], Y_ + 56, F32R)
        up_a = place("up_a", [P, DK, SEQ], Y_)
        up_b = place("up_b", [P, DK, SEQ], Y_ + 16)
        mg_hi = place("mg_hi", [P, DK, SEQ], Y_ + 32, F32R)
        mg_lo = place("mg_lo", [P, DK, SEQ], Y_ + 48, F32R)
        dist = place("dist", [P, SEQ], Y_ + 48)
        dist_i = place("dist_i", [P, SEQ], Y_ + 50, I32)
        far_neg = place("far_neg", [P, 3, SEQ], Y_ + 52)
        ps = ctx.enter_context(nc.psum_tensor("ps", [P, 8, 512], F32))
        ps_flat = ps[:, :, :].rearrange("p b c -> p (b c)")

        def sem(name):
            return ctx.enter_context(nc.semaphore(name))

        w_loaded = [sem("w_loaded_even"), sem("w_loaded_odd")]
        w_hi_ready, w_lo_ready = sem("w_hi_ready"), sem("w_lo_ready")
        mm_done, bank_free = sem("mm_done"), sem("bank_free")
        acc_free, h2_ready = sem("acc_free"), sem("h2_ready")
        x_loaded, consts_loaded = sem("x_loaded"), sem("consts_loaded")
        e_loaded, rows_loaded = sem("e_loaded"), sem("rows_loaded")
        sgu_loaded = sem("sgu_loaded")
        squares, rstd_ready, xs_ready = sem("squares"), sem("rstd_ready"), sem("xs_ready")
        xt_done, x_hi_ready, x_ready, xt_value = sem("xt_done"), sem("x_hi_ready"), sem("x_ready"), sem("xt_value")
        m_added = sem("m_added")
        act_chain, dve_chain, pool_chain = sem("act_chain"), sem("dve_chain"), sem("pool_chain")
        consts_made, e_masks, s_masks = sem("consts_made"), sem("e_masks"), sem("s_masks")
        gates_raw, gates_added = sem("gates_raw"), sem("gates_added")
        cmp_mm, cmp_act = sem("cmp_mm"), sem("cmp_act")
        gla_mm, gla_pre, gla_log, gla_exp, gla_ops = sem("gla_mm"), sem("gla_pre"), sem("gla_log"), sem("gla_exp"), sem("gla_ops")
        gla_a, gla_am, gla_ket, gla_ds, gla_s, gla_o, gla_oe = (sem(x) for x in (
            "gla_a", "gla_am", "gla_ket", "gla_ds", "gla_s", "gla_o", "gla_oe"))
        gn_sq, gn_mm, gn_ms, gn_rs, gn_done = (sem(x) for x in ("gn_sq", "gn_mm", "gn_ms", "gn_rs", "gn_done"))
        sc_done, mx_done, ex_done, pr_done, tr_done, pt_done, pv_done, o_done = (sem(x) for x in (
            "sc_done", "mx_done", "ex_done", "pr_done", "tr_done", "pt_done", "pv_done", "o_done"))
        ln_stat, ln_rstd, ln_done = sem("ln_stat"), sem("ln_rstd"), sem("ln_done")
        ws_mm, ws_copied, mix_mm, mix_evac, y_ready = (sem(x) for x in ("ws_mm", "ws_copied", "mix_mm", "mix_evac", "y_ready"))
        f_made, f_sum, up_ready = sem("f_made"), sem("f_sum"), sem("up_ready")
        ada_loaded = [sem("ada_loaded0"), sem("ada_loaded1")]
        ada_sum, ada_mm, ada_mod, c_ready = sem("ada_sum"), sem("ada_mm"), sem("ada_mod"), sem("c_ready")
        h_ready, gate_used, y_value, y_hi_ready, cmp_loaded, cmp_x_ready, cmp_step = (sem(x) for x in (
            "h_ready", "gate_used", "y_value", "y_hi_ready", "cmp_loaded", "cmp_x_ready", "cmp_step"))
        final_done, stored = sem("final_done"), sem("stored")

        def rows(w):
            return w.rearrange("(k p) c -> p k c", p=P)

        w_e, w_eo = rows(A["e_w_in"][0]), rows(A["e_w_out"][0])
        w_f1, w_f2 = [rows(A["ffn_w1"][l]) for l in range(2)], [rows(A["ffn_w2"][l]) for l in range(2)]
        w_o, w_oo = rows(A["o_w_in"][0]), rows(A["o_w_out"][0])
        w_s2, w_out2 = rows(A["w_in_2"][0]), rows(A["w_out_2"][0])
        w_ua, w_ub = rows(A["w_up_a_2"][0]), rows(A["w_up_b_2"][0])
        w_g1, w_g2 = rows(A["w_ffn_in_2"][0]), rows(A["w_ffn_out_2"][0])

        def by8(t, s):
            return t[:, s, :].rearrange("p (k c) -> p k c", k=8)

        def by2(t, s):
            return t[:, s, :].rearrange("p (k c) -> p k c", k=2)

        PASSES = ["e_out", "f0_down0", "f0_down1", "f0_down2", "o_out", "f1_down0", "f1_down1",
                  "f1_down2", "s_out", "g_down0", "g_down1"]
        def h2_base(name):
            base = {"f0_0": 0, "f0_1": 12, "f0_2": 24, "f1_0": 32, "f1_1": 44, "f1_2": 56, "g_0": 64, "g_1": 76}
            return base[name]

        def sum_done(pass_no, t):
            st = S[PASSES[pass_no]]
            return st.done + st.count - 1 + t + 1

        m_adds = {2: 0, 3: 4, 6: 8, 7: 12, 10: 16}
        U_NSA, U_DIL, U_FOX = 0, 32, 48

        def nsa_tiles(t):
            return 1 + 2 * (t + 1)

        def dil_tiles(t):
            return min(2, t + 1) + 2 * (t + 1)

        def fox_tiles(t):
            return t + 1

        def groups(n):
            return (n + 3) // 4

        def small_scores(s, n):
            return ps[:, 4, 256 * s:256 * s + n]

        def out_bank(half):
            return ps[half * HD:(half + 1) * HD, 7, 0:P]

        G_NSA = 8 * sum(groups(nsa_tiles(t)) for t in range(NT))
        G_DIL = 4 * sum(groups(dil_tiles(t)) for t in range(NT))

        class Kind:

            def __init__(self, name, loops, unit, group, key_tiles):
                self.name, self.loops, self.unit, self.group, self.key_tiles = name, loops, unit, group, key_tiles
                self.units = 2 * NT
                self.groups = 2 * sum(groups(key_tiles(t)) for t in range(NT))

            def turns(self):
                g = 0
                for t in range(NT):
                    for half in range(2):
                        yield half, t, g
                        g += groups(self.key_tiles(t))

        nsa = Kind("nsa", 4, U_NSA, 0, nsa_tiles)
        dil = Kind("dil", 2, U_DIL, G_NSA, dil_tiles)
        fox = Kind("fox", 2, U_FOX, G_NSA + G_DIL, fox_tiles)

        def is_last(kind, it):
            return isinstance(it, int) and it == kind.loops - 1

        block = ctx.enter_context(nc.Block())

        @block.sync
        def _(sp):
            def load(n, slot, pieces):
                if not isinstance(n, int) or n >= 2:
                    sp.wait_ge(w_lo_ready, n - 1)
                for dst, src in pieces:
                    sp.dma_start(dst, src).then_inc(w_loaded[slot], 16)

            def load_cols(name, w, first_col):
                st = S[name]

                def body(i, q, it):
                    s = (st.first + q) % 2
                    load(i + st.first, s, [(by8(w_raw, s), w[:, :, bass.ds(i * 256 + first_col, 256)])])
                tiles(sp, st, body)

            def load_listed(name, w, cols):
                for i, c in enumerate(cols):
                    s = (S[name].first + i) % 2
                    load(S[name].first + i, s, [(by8(w_raw, s), w[:, :, c:c + 256])])

            def load_rows(name, w, first_chunk):
                st = S[name]

                def body(i, q, it):
                    s = (st.first + q) % 2
                    load(i + st.first, s, [(by2(w_raw, s), w[:, bass.ds(i * 2 + first_chunk, 2), :])])
                tiles(sp, st, body)

            def load_pairs(name, w, first_block):
                st = S[name]
                with sp.Fori(0, st.count // 2) as it:
                    for q, col in ((0, first_block * P), (1, DFF + first_block * P)):
                        s = (st.first + q) % 2
                        load(it * 2 + (st.first + q), s, [(by8(w_raw, s), w[:, :, bass.ds(it * 256 + col, 256)])])

            def row(src):
                sp.dma_start(row_gain[:, :], src.partition_broadcast(P)).then_inc(rows_loaded, 16)

            sp.dma_start(h[:, :, :], A["x"][0].rearrange("(t p) d -> p t d", p=P)).then_inc(x_loaded, 16)
            load_listed("e_cols", w_e, [GQ, GK, GR, GR + 256, NQ, NQ + 256, KC])
            two = [(S["e_cols"].first + 7, KS, KW), (S["e_v"].first + 2, VS, VW)]

            def load_two(n, a, b):
                s = n % 2
                load(n, s, [(by8(w_raw, s)[:, :, 0:P], w_e[:, :, a:a + P]),
                            (by8(w_raw, s)[:, :, P:2 * P], w_e[:, :, b:b + P])])
            load_two(*two[0])
            sp.wait_ge(xt_done, DK)
            for x in range(2):
                sp.dma_start(cmp_w1[x][:, :, :],
                             A["nsa_cmp_w1"][0, x].rearrange("(a q) h -> q a h", q=P)).then_inc(cmp_loaded, 16)
            n = S["e_small"].first
            s = n % 2
            load(n, s, [(by8(w_raw, s)[:, :, 0:P], w_e[:, :, GLR:GLR + P]),
                        (by8(w_raw, s)[:, :, P:P + NG_COLS], w_e[:, :, NG:NG + NG_COLS])])
            load_listed("e_v", w_e, [GV, GV + 256])
            load_two(*two[1])
            load_rows("e_out", w_eo, 0)
            sp.wait_ge(o_done, 2 + 32)
            row(A["norm_g"][0, 1])
            load_cols("f0_up0", w_f1[0], 0)

            def mlp_loads(l, rows_before, h_before, src):
                load_rows(f"f{l}_down0", w_f2[l], 0)
                sp.wait_ge(h_ready, h_before)
                row(src)
                load_cols(f"f{l}_up1", w_f1[l], 12 * P)
                load_rows(f"f{l}_down1", w_f2[l], 12)
                load_cols(f"f{l}_up2", w_f1[l], 24 * P)
                load_rows(f"f{l}_down2", w_f2[l], 24)

            mlp_loads(0, 1, 4, A["norm_g"][0, 3])
            load_cols("o_u", w_o, 0)
            sp.wait_ge(h_ready, 8)
            sp.dma_start(b_s_row[:, :, :].rearrange("p g t -> p (g t)"),
                         A["o_b_s"][0].rearrange("g t -> (g t)").partition_broadcast(P)).then_inc(sgu_loaded, 16)
            load_cols("o_v", w_o, SGU)
            load_rows("o_out", w_oo, 0)
            sp.wait_ge(y_ready, 16)
            row(A["norm_g"][1, 1])
            load_cols("f1_up0", w_f1[1], 0)
            mlp_loads(1, 3, 12, A["norm_g"][1, 3])
            load_listed("s_qk", w_s2, [QA, QA + 256, QA + 512, KA, KA + 256, KA + 512, QB, KB])
            load_listed("s_v", w_s2, [VA, VA + 256, VA + 512, VB])
            n = S["s_small"].first
            load(n, n % 2, [(by8(w_raw, n % 2)[:, :, 0:P], w_s2[:, :, FZ:FZ + P])])
            load_rows("s_upa", w_ua, 0)
            load_rows("s_upb", w_ub, 0)
            load_cols("s_ga", w_s2, GZA)
            load_cols("s_gb", w_s2, GZB)
            load_rows("s_out", w_out2, 0)
            load_pairs("g_up0", w_g1, 0)
            row(A["norm_final_2"])
            load_rows("g_down0", w_g2, 0)
            load_pairs("g_up1", w_g1, 12)
            load_rows("g_down1", w_g2, 12)
            for t in range(NT):
                sp.wait_ge(final_done, t + 1)
                sp.dma_start(out[0].rearrange("(t p) d -> p t d", p=P)[:, t, :],
                             m[:, t, :]).then_inc(stored, 16)
            sp.wait_ge(stored, 16 * NT)

        @block.gpsimd
        def _(pool):
            chain = Chain(pool, pool_chain)

            nc.gpsimd.memset(ident[:, :], 0.0).then_inc(pool_chain, 1)
            nc.gpsimd.memset(causal[:, :], 0.0).then_inc(pool_chain, 1)
            nc.gpsimd.memset(gla_mask[:, :], 1.0).then_inc(pool_chain, 1)
            nc.gpsimd.memset(keep[:, :], 1.0).then_inc(pool_chain, 1)
            nc.gpsimd.memset(cmp_add[:, :, :], 0.0).then_inc(pool_chain, 1)
            nc.gpsimd.memset(cmp_one[:, :, :], 1.0).then_inc(pool_chain, 1)
            chain.n = 6
            chain.link(nc.gpsimd.memset(neg_half[:, :], -0.5))
            chain.link(nc.gpsimd.affine_select(out=ident[:, :], in_=ident[:, :], compare_op=ALU.not_equal, fill=1.0,
                                               base=0, pattern=[[-1, P]], channel_multiplier=1))
            chain.link(nc.gpsimd.affine_select(out=causal[:, :], in_=causal[:, :], compare_op=ALU.is_ge, fill=NEG,
                                               base=0, pattern=[[-1, P]], channel_multiplier=1))
            nc.gpsimd.memset(ones[:, :], 1.0).then_inc(consts_made, 1)

            n_squares = [0]

            def rstds(count):
                for _ in range(count):
                    e = n_squares[0]
                    n_squares[0] += 1
                    c = e % 16
                    pool.wait_ge(squares, e + 1)
                    chain.link(nc.gpsimd.tensor_scalar(ss[:, c:c + 1], ss[:, c:c + 1], EPS, None, ALU.add))
                    nc.gpsimd.tensor_tensor(rstd[:, c:c + 1], ss[:, c:c + 1], neg_half[:, 0:1],
                                            ALU.pow).then_inc(rstd_ready, 1)

            rstds(4)
            chain.link(nc.gpsimd.affine_select(out=gla_mask[:, :], in_=gla_mask[:, :], compare_op=ALU.is_ge, fill=0.0,
                                               base=0, pattern=[[1, P]], channel_multiplier=-1))
            chain.link(nc.gpsimd.affine_select(out=gla_mask[:, CH:P], in_=gla_mask[:, CH:P], compare_op=ALU.is_ge,
                                               fill=0.0, base=-CH, pattern=[[0, CH]], channel_multiplier=1))
            nc.gpsimd.memset(am[:, :, :, :], 0.0)
            nc.gpsimd.memset(v_cmp[:, :, :], 0.0)
            for t in range(NT):
                for tile_, fill in ((cmp_add, NEG), (cmp_one, 0.0)):
                    nc.gpsimd.affine_select(out=tile_[:, t, :], in_=tile_[:, t, :], compare_op=ALU.is_ge, fill=fill,
                                            base=P * t - (CMP_BLOCK - 1), pattern=[[-CMP_STRIDE, 32]],
                                            channel_multiplier=1)
            nc.gpsimd.memset(keep[:, 0:SEQ:CH], 0.0).then_inc(e_masks, 1)
            pool.wait_ge(cmp_mm, 1)
            nc.gpsimd.memset(prob_n[:, :, 0:P], 0.0).then_inc(e_masks, 1)

            rstds(8)

            ada_n = [0, 0]

            def ada_chunk(cc):
                if cc:
                    pool.wait_ge(ada_mm, cc)
                for k in range(DK):
                    s = k % 2
                    pool.dma_start(ada_w[:, s, :], A["w_ada_2"][0, k * P:(k + 1) * P, cc * 1024:(cc + 1) * 1024])\
                        .then_inc(ada_loaded[s], 16)
                    if k:
                        ada_use(k - 1)
                ada_use(DK - 1)

            def ada_use(k):
                s = k % 2
                ada_n[s] += 16
                pool.wait_ge(ada_loaded[s], ada_n[s])
                if k == 0:
                    chain.link(nc.gpsimd.tensor_scalar(ada_acc[:, :], ada_w[:, s, :], c_col[:, k:k + 1], None, ALU.mult))
                    return
                chain.link(nc.gpsimd.tensor_scalar(ada_w[:, s, :], ada_w[:, s, :], c_col[:, k:k + 1], None, ALU.mult))
                add = nc.gpsimd.tensor_tensor(ada_acc[:, :], ada_acc[:, :], ada_w[:, s, :], ALU.add)
                chain.link(add)
                if k == DK - 1:
                    pool.sem_inc(ada_sum, 1)

            pool.wait_ge(c_ready, 1)
            for cc in range(5):
                ada_chunk(cc)
            rstds(8)
            pool.wait_ge(sgu_loaded, 16)
            for g in range(8):
                last_ = nc.gpsimd.affine_select(out=w_s[:, g, :], in_=w_s[:, g, :], compare_op=ALU.is_ge,
                                                fill=0.0, base=0, pattern=[[-1, P]], channel_multiplier=1)
            last_.then_inc(s_masks, 1)
            for t in range(NT):
                pool.wait_ge(ln_stat, t + 1)
                chain.link(nc.gpsimd.tensor_scalar(mv[:, t, 1:2], mv[:, t, 1:2], EPS, None, ALU.add))
                nc.gpsimd.tensor_tensor(mv[:, t, 1:2], mv[:, t, 1:2], neg_half[:, 0:1],
                                        ALU.pow).then_inc(ln_rstd, 1)
            rstds(8)
            ada_chunk(5)
            rstds(8)
            pool.wait_ge(mm_done, S["s_v"].done)
            nc.gpsimd.iota(dist_i[:, :], pattern=[[-1, SEQ]], base=SEQ - P, channel_multiplier=1)\
                .then_inc(f_made, 1)
            pool.wait_ge(f_made, 2)
            for g in range(3):
                chain.link(nc.gpsimd.affine_select(out=far_neg[:, g, :], in_=far_neg[:, g, :],
                                                   compare_op=ALU.is_ge, fill=NEG, base=SEQ - P,
                                                   pattern=[[-1, SEQ]], channel_multiplier=1))
            nc.gpsimd.affine_select(out=far_neg[:, 0, :], in_=far_neg[:, 0, :], compare_op=ALU.is_ge, fill=NEG,
                                    base=DILATED[0][0] - (SEQ - P), pattern=[[1, SEQ]],
                                    channel_multiplier=-1).then_inc(f_made, 1)
            rstds(4)
            rstds(4)

        @block.scalar
        def _(act):
            chain = Chain(act, act_chain)

            def split_hi(n, slot, arrived, used):
                act.wait_ge(w_loaded[slot], arrived)
                if not isinstance(used, int) or used > 0:
                    act.wait_ge(mm_done, used)
                nc.scalar.activation(w_hi[:, slot, :], w_raw[:, slot, :], ACT.Copy).then_inc(w_hi_ready, 1)

            def split_next(st, i, q, it):
                n = st.first + q + 1
                if isinstance(i, int) and st.first + i + 1 >= N_TILES:
                    return
                if isinstance(i, int) and isinstance(it, int):
                    n = st.first + i + 1
                    split_hi(n, n % 2, loaded(n), i * st.per + st.done)
                else:
                    split_hi(i + (st.first + 1), n % 2, it * (loaded(n + 2) - loaded(n)) + loaded(n),
                             i * st.per + st.done)

            def unit_wait(st, i, f, per=2):
                act.wait_ge(mm_done, i * per + (st.done + f + 1))

            def bank(st, q, f):
                return (st.unit + 2 * q + f) % 4

            def take_up(name, body):
                st = S[name]

                def turn(i, q, it):
                    split_next(st, i, q, it)
                    for f in range(2):
                        unit_wait(st, i, f)
                        body(i, q, f, bank(st, q, f))
                tiles(act, st, turn)

            def splits(name):
                tiles(act, S[name], lambda i, q, it: split_next(S[name], i, q, it))

            def square_m(t, e, src, dst):
                c = e % 16
                return nc.scalar.activation(dst, src, ACT.Square, scale=1.0 / 32.0, accum_out=ss[:, c:c + 1])

            def h_squares(e):
                for t in range(NT):
                    square_m(t, e + t, h[:, t, :], m[:, t, :]).then_inc(squares, 1)

            def transposed_hi(p):
                for k in range(DK):
                    if p < 4:
                        act.wait_ge(xt_done, DK * p + k + 1)
                        src, gain = ps[:, k, :], col_gain[:, p, k:k + 1]
                        nc.scalar.activation(x_hi[:, k, :], src, ACT.Copy, scale=gain).then_inc(x_hi_ready, 1)
                    else:
                        act.wait_ge(xt_value, DK * (p - 4) + k + 1)
                        nc.scalar.activation(x_hi[:, k, :], work[:, k % 2, :], ACT.Copy).then_inc(x_hi_ready, 1)

            def bank_pair(t):
                return ps_flat[:, t * 1024:(t + 1) * 1024]

            def post(pass_no, e, partial, h_before, p):
                for t in range(NT):
                    if partial:
                        act.wait_ge(m_added, m_adds[pass_no] + t + 1)
                    else:
                        act.wait_ge(mm_done, sum_done(pass_no, t))
                        chain.link(nc.scalar.activation(m[:, t, :], bank_pair(t), ACT.Copy))
                    square_m(t, e + t, m[:, t, :], bank_pair(t)).then_inc(squares, 1)
                for t in range(NT):
                    act.wait_ge(h_ready, h_before + t + 1)
                    square_m(t, e + NT + t, h[:, t, :], m[:, t, :]).then_inc(squares, 1)

            def copy_sum(pass_no):
                for t in range(NT):
                    act.wait_ge(mm_done, sum_done(pass_no, t))
                    nc.scalar.activation(m[:, t, :], bank_pair(t), ACT.Copy).then_inc(acc_free, 1)

            def cload(dst, src, s=consts_loaded):
                act.dma_start(dst, src, allow_slow_non_contiguous=True).then_inc(s, 16)

            cload(col_gain[:, 0, :], A["norm_g"][0, 0].rearrange("(k p) -> p k", p=P))
            cload(col_gain[:, 1, :], A["norm_g"][0, 2].rearrange("(k p) -> p k", p=P))
            cload(col_gain[:, 2, :], A["norm_g"][1, 0].rearrange("(k p) -> p k", p=P))
            cload(col_gain[:, 3, :], A["norm_g"][1, 2].rearrange("(k p) -> p k", p=P))
            cload(col_gain[:, 4, :], A["norm_mix_2"][0].rearrange("(k p) -> p k", p=P))
            cload(col_gain[:, 5, :], A["norm_ffn_2"][0].rearrange("(k p) -> p k", p=P))
            cload(c_col[:, :], A["c_2"][0].rearrange("(k p) -> p k", p=P))
            cload(b_ada_col[:, :], A["b_ada_2"][0].rearrange("(k p) -> p k", p=P))
            cload(g1_row[:, :], A["b_ada_2"][0, 2048:3072].partition_broadcast(P))
            cload(g2_row[:, :], A["b_ada_2"][0, 5120:6144].partition_broadcast(P))
            cload(ln_g_col[:, :], A["o_ln_g"][0].rearrange("(k p) -> p k", p=P))
            cload(ln_b_col[:, :], A["o_ln_b"][0].rearrange("(k p) -> p k", p=P))
            cload(b_forget[:, :], A["b_forget_2"][0].rearrange("(k o) -> k o", o=1))
            N_CONSTS = 13
            cload(w_gate[0:RANK, :], A["gla_w_gate"][0], e_loaded)
            cload(b_gate[:, :], A["gla_b_gate"][0].rearrange("(k p) -> p k", p=P), e_loaded)
            cload(gla_norm[:, :], A["gla_norm"][0].rearrange("h v -> v h"), e_loaded)
            cload(gate_rows[:, :], A["nsa_gate_b"][0].partition_broadcast(P), e_loaded)
            for x in range(2):
                for par in range(2):
                    src = A["nsa_cmp_pos"][0, x].rearrange("(a b) d -> b d a", b=2)
                    cload(cmp_pos[par * HD:(par + 1) * HD, x, :], src[par], e_loaded)
                cload(cmp_w2[:, x, :], A["nsa_cmp_w2"][0, x], e_loaded)
            N_E = 10

            act.wait_ge(x_loaded, 16)
            nc.scalar.activation(small[:, 0:1], h[:, 0, 0:1], ACT.Copy).then_inc(bank_free, 4)
            nc.scalar.activation(small[:, 1:2], h[:, 0, 0:1], ACT.Copy).then_inc(ex_done, 2)
            nc.scalar.activation(small[:, 2:3], h[:, 0, 0:1], ACT.Copy).then_inc(pt_done, 2)
            h_squares(0)
            split_hi(0, 0, loaded(0), 0)
            act.wait_ge(consts_loaded, 16 * N_CONSTS)
            transposed_hi(0)

            st = S["e_cols"]
            for i in range(8):
                split_next(st, i, 0, i // 2)
                for f in range(2):
                    u, b_ = 2 * i + f, (st.unit + 2 * i + f) % 4
                    act.wait_ge(mm_done, st.done + u + 1)
                    src = ps[:, b_, :]
                    if u < 2 or 8 <= u < 12:
                        o = nc.scalar.activation(e_t[:, u, :], src, ACT.Copy, scale=HD ** -0.5)
                    elif u < 4:
                        o = nc.scalar.activation(e_t[:, u, :], src, ACT.Copy)
                    elif u < 8:
                        o = nc.scalar.activation(e_t[:, u, :], src, ACT.Silu)
                    elif u < 14:
                        x = u - 12
                        for g in range(2):
                            lo = ps[g * HD:(g + 1) * HD, b_, :]
                            nc.scalar.activation(x_c[0:HD, 2 * x + g, :], lo, ACT.Copy)
                            o = nc.scalar.activation(x_c[HD:P, 2 * x + g, 0:SEQ - 1], lo[:, 1:SEQ], ACT.Copy)
                    else:
                        k_dst = k_s if u == 14 else k_w
                        for g in range(2):
                            for half in range(2):
                                o = nc.scalar.activation(k_dst[half * HD:(half + 1) * HD, g, :],
                                                         ps[g * HD:(g + 1) * HD, b_, :], ACT.Copy)
                    o.then_inc(bank_free, 1)
            st = S["e_small"]
            split_next(st, 0, 0, 0)
            act.wait_ge(mm_done, st.done + 1)
            nc.scalar.activation(f_row[0:RANK, :], ps[0:RANK, st.unit % 4, :], ACT.Copy).then_inc(bank_free, 1)
            act.wait_ge(mm_done, st.done + 2)
            nc.scalar.activation(branch_gate[:, :, :],
                                 ps[:, (st.unit + 1) % 4, 0:NT * NG_COLS].rearrange("p (t c) -> p t c", t=NT),
                                 ACT.Copy).then_inc(bank_free, 1)
            for b_ in range(2):
                act.wait_ge(gla_mm, b_ + 1)
                chain.link(nc.scalar.activation(cum[:, b_, :], ps[:, 6 + b_, :], ACT.Identity, bias=b_gate[:, b_:b_ + 1]))
                chain.link(nc.scalar.activation(t1[:, b_, :], cum[:, b_, :], ACT.Abs))
                chain.link(nc.scalar.activation(t1[:, b_, :], t1[:, b_, :], ACT.Exp, scale=-1.0))
                chain.link(nc.scalar.activation(t1[:, b_, :], t1[:, b_, :], ACT.Ln, bias=1.0))
                act.sem_inc(gla_pre, 1)
            def take_v(i):
                st = S["e_v"]
                split_next(st, i, 0, i // 2)
                for f in range(2):
                    act.wait_ge(mm_done, st.done + 2 * i + f + 1)
                    src = ps[:, (st.unit + 2 * i + f) % 4, :].rearrange("p (t c) -> p t c", t=2)
                    dst = g_v[:, 2 * f:2 * f + 2, 256 * i:256 * i + 256] if i < 2 else v_sw[:, 2 * f:2 * f + 2, :]
                    nc.scalar.activation(dst, src, ACT.Copy).then_inc(bank_free, 1)

            take_v(0)
            for b_ in range(2):
                act.wait_ge(gla_log, 2 * b_ + 1)
                nc.scalar.activation(chunk_decay[:, b_, :], cum[:, b_, CH - 1:SEQ:CH], ACT.Exp)
                nc.scalar.activation(t1[:, b_, :], cum[:, b_, :], ACT.Exp).then_inc(gla_exp, 1)
                act.wait_ge(gla_ops, 2 * b_ + 1)
                nc.scalar.activation(t1[:, b_, :], cum[:, b_, :], ACT.Exp, scale=-1.0).then_inc(gla_exp, 1)
                act.wait_ge(gla_log, 2 * b_ + 2)
                nc.scalar.activation(k_end[:, b_, :], k_end[:, b_, :], ACT.Exp).then_inc(gla_exp, 1)

            take_v(1)
            take_v(2)
            act.wait_ge(gates_added, 1)
            nc.scalar.activation(branch_gate[:, :, :], branch_gate[:, :, :], ACT.Sigmoid).then_inc(gates_raw, 1)

            act.wait_ge(cmp_mm, 1)
            nc.scalar.activation(cmp_hid[:, :, 0:CMP_N], ps[:, 4, 0:4 * CMP_N].rearrange("p (c n) -> p c n", c=4),
                                 ACT.Gelu_apprx_tanh).then_inc(cmp_act, 1)
            act.wait_ge(e_masks, 2)
            act.wait_ge(cmp_mm, 2)
            nc.scalar.activation(k_cmp[:, :, 0:CMP_N],
                                 ps[:, 5, 0:64].rearrange("p (g c) -> p g c", g=2)[:, :, 0:CMP_N], ACT.Copy)
            nc.scalar.activation(v_cmp[0:CMP_N, :, :], ps[0:CMP_N, 5, 64:192].rearrange("p (g c) -> p g c", g=2),
                                 ACT.Copy).then_inc(cmp_act, 1)

            for v in range(8):
                b_, t = divmod(v, 4)
                act.wait_ge(gla_a, v + 1)
                nc.scalar.activation(k_end_t[:, v % 2, :], ps[:, 6 + v % 2, 0:P], ACT.Copy).then_inc(gla_ket, 1)
                act.wait_ge(gla_o, v + 1)
                nc.scalar.activation(o_gla[:, 2 * b_:2 * b_ + 2, t * P:(t + 1) * P],
                                     ps[:, 4:6, 0:P],
                                     ACT.Copy).then_inc(gla_oe, 1)
            act.wait_ge(gla_oe, 8)
            for hd in range(GLA_HEADS):
                nc.scalar.activation(cum[:, hd % 2, :] if hd < 2 else state_flat[:, hd % 2, :], o_gla[:, hd, :],
                                     ACT.Square).then_inc(gn_sq, 1)
            for hd in range(GLA_HEADS):
                act.wait_ge(gn_ms, hd + 1)
                if hd >= 2:
                    act.wait_ge(gn_done, hd - 1)
                nc.scalar.activation(t1[:, hd % 2, :], gn_inv[:, hd % 2, :], ACT.Sqrt).then_inc(gn_rs, 1)

            def exps_nsa(s, t):
                nk = P * (t + 1)
                st_ = att_stat[:, s, :]
                nc.scalar.activation(prob_n[:, s, 0:CMP_N], small_scores(s, CMP_N), ACT.Exp,
                                     bias=st_[:, 3:4])
                nc.scalar.activation(prob_n[:, s, P:P + nk], ps[:, 2 * s, 0:nk], ACT.Exp,
                                     bias=st_[:, 4:5], accum_out=st_[:, 7:8])
                return nc.scalar.activation(prob_n[:, s, P + nk:P + 2 * nk], ps[:, 2 * s + 1, 0:nk], ACT.Exp,
                                            bias=st_[:, 5:6], accum_out=st_[:, 8:9])

            def exps_dil(s, t):
                nk, n0 = P * (t + 1), P * min(2, t + 1)
                st_ = att_stat[:, s, :]
                nc.scalar.activation(prob[:, s, 0:n0], small_scores(s, n0), ACT.Exp,
                                     bias=st_[:, 4:5], accum_out=st_[:, 7:8])
                nc.scalar.activation(prob[:, s, n0:n0 + nk], ps[:, 2 * s, 0:nk], ACT.Exp,
                                     bias=st_[:, 4:5], accum_out=st_[:, 8:9])
                return nc.scalar.activation(prob[:, s, n0 + nk:n0 + 2 * nk], ps[:, 2 * s + 1, 0:nk], ACT.Exp,
                                            bias=st_[:, 4:5], accum_out=st_[:, 9:10])

            def exps_fox(s, t):
                nk = P * (t + 1)
                st_ = att_stat[:, s, :]
                return nc.scalar.activation(prob[:, s, 0:nk], ps[:, 2 * s, 0:nk], ACT.Exp,
                                            bias=st_[:, 4:5], accum_out=st_[:, 7:8])

            def attention(kind, exps):
                order_ = list(kind.turns())

                def exp_unit(su, it):
                    half, t, g0 = order_[su % kind.units]
                    act.wait_ge(mx_done, it * kind.units + (kind.unit + su + 1))
                    exps(su % 2, t).then_inc(ex_done, 1)

                def body(it):
                    for su, (half, t, g0) in enumerate(order_):
                        n = kind.key_tiles(t)
                        for g in range(groups(n)):
                            width = P * min(4, n - 4 * g)
                            act.wait_ge(tr_done, it * kind.groups + (kind.group + g0 + g + 1))
                            nc.scalar.activation(prob_t[:, (g0 + g) % 2, 0:width], ps[:, 5 + (g0 + g) % 2, 0:width],
                                                 ACT.Copy).then_inc(pt_done, 1)
                            if g == 0 and not (is_last(kind, it) and su == kind.units - 1):
                                exp_unit(su + 1, it)

                exp_unit(0, 0)
                with act.Fori(0, kind.loops - 1) as it:
                    body(it)
                body(kind.loops - 1)

            attention(nsa, exps_nsa)
            splits("e_out")
            post(0, 4, False, 0, 1)

            def mlp_up(l, part):
                st, base = S[f"f{l}_up{part}"], h2_base(f"f{l}_{part}")

                def turn(i, q, it):
                    split_next(st, i, q, it)
                    for f in range(2):
                        unit_wait(st, i, f)
                        act.wait_ge(h2_ready, i * 2 + (base + f + 1))
                        nc.scalar.activation(work[:, f, :], ps[:, bank(st, q, f), :], ACT.Relu).then_inc(bank_free, 1)
                tiles(act, st, turn)

            def mlp_layer(l, first_pass, e):
                transposed_hi(1 if l == 0 else 3)
                mlp_up(l, 0)
                splits(f"f{l}_down0")
                copy_sum(first_pass)
                mlp_up(l, 1)
                splits(f"f{l}_down1")
                mlp_up(l, 2)
                splits(f"f{l}_down2")
                post(first_pass + 2, e, True, {0: 4, 1: 12}[l], None)

            nc.scalar.activation(c_col[:, :], c_col[:, :], ACT.Silu).then_inc(c_ready, 1)
            mlp_layer(0, 1, 12)

            act.dma_start(w_s[:, :, :], A["o_w_s"][0].rearrange("g t s -> t g s")).then_inc(sgu_loaded, 16)
            transposed_hi(2)
            for half in range(2):
                act.wait_ge(ws_mm, half + 1)
                nc.scalar.activation(w_st[:, 4 * half:4 * half + 4, :].rearrange("p g t -> p (g t)"),
                                     ps[:, 4 + half, :], ACT.Copy).then_inc(ws_copied, 1)
            for half in range(2):
                act.wait_ge(ws_mm, half + 3)
                nc.scalar.activation(w_sum[:, 4 * half:4 * half + 4, :].rearrange("p g t -> p (g t)"),
                                     ps[:, 6 + half, :], ACT.Copy).then_inc(ws_copied, 1)

            def gelu_u(i, q, f, b_):
                nc.scalar.activation(u_t[:, bass.ds(i * 2 + f, 1), :], ps[:, b_:b_ + 1, :],
                                     ACT.Gelu_apprx_tanh).then_inc(bank_free, 1)
            take_up("o_u", gelu_u)

            def gelu_v(i, q, f, b_):
                nc.scalar.activation(v_ln[:, 2 * f:2 * f + 2, bass.ds(i * 256, 256)],
                                     ps[:, b_, :].rearrange("p (t c) -> p t c", t=2),
                                     ACT.Gelu_apprx_tanh).then_inc(bank_free, 1)
            take_up("o_v", gelu_v)
            for f in range(16):
                act.wait_ge(y_value, f + 1)
                nc.scalar.activation(y_hi[:, f, :], work[:, f % 2, :], ACT.Copy).then_inc(y_hi_ready, 1)
            splits("o_out")
            post(4, 20, False, 8, 3)

            mlp_layer(1, 5, 28)

            transposed_hi(4)
            st = S["s_qk"]
            for i in range(8):
                split_next(st, i, 0, i // 2)
                for f in range(2):
                    u = 2 * i + f
                    act.wait_ge(mm_done, st.done + u + 1)
                    scale = HD ** -0.5 if u < 6 or u in (12, 13) else 1.0
                    nc.scalar.activation(q_k[:, u, :], ps[:, (st.unit + u) % 4, :], ACT.Copy,
                                         scale=scale).then_inc(bank_free, 1)

            def copy_v(i, q, f, b_):
                nc.scalar.activation(v_ab[:, 2 * f:2 * f + 2, bass.ds(i * 256, 256)],
                                     ps[:, b_, :].rearrange("p (t c) -> p t c", t=2),
                                     ACT.Copy).then_inc(bank_free, 1)
            take_up("s_v", copy_v)
            st = S["s_small"]
            split_next(st, 0, 0, 0)
            act.wait_ge(mm_done, st.done + 1)
            fa, fb = f_row[0:4, :], prob[0:4, 0, 0:SEQ]
            nc.scalar.activation(fa, ps[0:4, st.unit % 4, :], ACT.Identity, bias=b_forget[:, 0:1]).then_inc(bank_free, 1)
            chain.link(nc.scalar.activation(fb, ps[0:4, st.unit % 4, :], ACT.Abs, bias=b_forget[:, 0:1]))
            chain.link(nc.scalar.activation(fb, fb, ACT.Exp, scale=-1.0))
            nc.scalar.activation(fb, fb, ACT.Ln, bias=1.0).then_inc(f_sum, 1)
            attention(dil, exps_dil)
            attention(fox, exps_fox)

            for name, dst in (("s_upa", up_a), ("s_upb", up_b)):
                st = S[name]
                split_next(st, 0, 0, 0)
                for f in range(DK):
                    act.wait_ge(mm_done, st.done + f + 1)
                    nc.scalar.activation(dst[:, f, :], ps[:, (st.unit + f) % 4, :], ACT.Copy).then_inc(bank_free, 1)

            for name, base in (("s_ga", 0), ("s_gb", DK)):
                st = S[name]

                def turn(i, q, it, st=st, base=base):
                    split_next(st, i, q, it)
                    for f in range(2):
                        unit_wait(st, i, f)
                        act.wait_ge(gate_used, i * 2 + (base + f + 1))
                        nc.scalar.activation(work[:, f, :], ps[:, bank(st, q, f), :],
                                             ACT.Sigmoid).then_inc(bank_free, 1)
                tiles(act, st, turn)
            splits("s_out")
            for t in range(NT):
                act.wait_ge(h_ready, 16 + t + 1)
                square_m(t, 36 + t, h[:, t, :], m[:, t, :]).then_inc(squares, 1)

            transposed_hi(5)
            for part in range(2):
                st, base, up_base = S[f"g_up{part}"], h2_base(f"g_{part}"), 12 * part

                def turn(i, q, it, st=st, base=base, up_base=up_base):
                    split_next(st, i, q, it)
                    for f in range(2):
                        if q == 0:
                            unit_wait(st, i, f)
                            act.wait_ge(h2_ready, it * 2 + (base + f + 1))
                            nc.scalar.activation(work[:, f, :], ps[:, bank(st, q, f), :],
                                                 ACT.Silu).then_inc(bank_free, 1)
                        else:
                            act.wait_ge(up_ready, it * 2 + (up_base + f + 1))
                            act.sem_inc(bank_free, 1)
                tiles(act, st, turn)
                splits(f"g_down{part}")
                if part == 0:
                    copy_sum(9)
            for t in range(NT):
                act.wait_ge(h_ready, 20 + t + 1)
                square_m(t, 40 + t, h[:, t, :], m[:, t, :]).then_inc(squares, 1)

        @block.vector
        def _(dve):
            chain = Chain(dve, dve_chain)

            def split_lo(n, slot):
                dve.wait_ge(w_hi_ready, n + 1)
                nc.vector.tensor_tensor(w_lo[:, slot, :], w_raw[:, slot, :], w_hi[:, slot, :].bitcast(F32),
                                        ALU.subtract).then_inc(w_lo_ready, 1)

            def split_next(st, i, q):
                if isinstance(i, int) and st.first + i + 1 >= N_TILES:
                    return
                split_lo(i + (st.first + 1), (st.first + q + 1) % 2)

            def splits(name):
                tiles(dve, S[name], lambda i, q, it: split_next(S[name], i, q))

            def taken(st, i, f, per=2):
                dve.wait_ge(bank_free, i * per + (4 + st.unit + f + 1))

            def bank_pair(t):
                return ps_flat[:, t * 1024:(t + 1) * 1024]

            def normed(e):
                for t in range(NT):
                    c = (e + t) % 16
                    dve.wait_ge(rstd_ready, e + t + 1)
                    nc.vector.tensor_scalar(m[:, t, :], h[:, t, :], rstd[:, c:c + 1], None, ALU.mult)\
                        .then_inc(xs_ready, 1)

            def transposed_lo(p):
                if p < 4:
                    for k in range(DK):
                        dve.wait_ge(x_hi_ready, DK * p + k + 1)
                        nc.vector.scalar_tensor_tensor(x_lo[:, k, :], ps[:, k, :], col_gain[:, p, k:k + 1],
                                                       x_hi[:, k, :].bitcast(F32), ALU.mult, ALU.subtract)\
                            .then_inc(x_ready, 1)
                    return

                def value(k):
                    dve.wait_ge(xt_done, DK * p + k + 1)
                    nc.vector.tensor_scalar(work[:, k % 2, :], ps[:, k, :], col_gain[:, p, k:k + 1],
                                            col_bias[:, p - 4, k:k + 1], ALU.mult, ALU.add).then_inc(xt_value, 1)
                value(0)
                for k in range(DK):
                    if k + 1 < DK:
                        if k:
                            dve.wait_ge(x_ready, DK * p + k)
                        value(k + 1)
                    dve.wait_ge(x_hi_ready, DK * p + k + 1)
                    nc.vector.tensor_tensor(x_lo[:, k, :], work[:, k % 2, :], x_hi[:, k, :].bitcast(F32),
                                            ALU.subtract).then_inc(x_ready, 1)

            def post(pass_no, e, partial, row_no):
                if partial:
                    add_sum(pass_no, False)
                dve.wait_ge(rows_loaded, 16 * row_no)
                for t in range(NT):
                    c = (e + t) % 16
                    dve.wait_ge(rstd_ready, e + t + 1)
                    chain.link(nc.vector.scalar_tensor_tensor(m[:, t, :], m[:, t, :], rstd[:, c:c + 1],
                                                              row_gain[:, :], ALU.mult, ALU.mult))
                    nc.vector.tensor_tensor(h[:, t, :], h[:, t, :], m[:, t, :], ALU.add).then_inc(h_ready, 1)
                normed(e + NT)

            def add_sum(pass_no, free):
                for t in range(NT):
                    dve.wait_ge(mm_done, sum_done(pass_no, t))
                    add = nc.vector.tensor_tensor(m[:, t, :], m[:, t, :], bank_pair(t), ALU.add)
                    add.then_inc(m_added, 1)
                    if free:
                        dve.wait_ge(m_added, m_adds[pass_no] + t + 1)
                        dve.sem_inc(acc_free, 1)

            nc.vector.memset(small[:, 16:17], 0.0).then_inc(h2_ready, 2)
            nc.vector.memset(small[:, 17:18], 0.0).then_inc(gate_used, 2)
            nc.vector.memset(small[:, 18:19], 0.0).then_inc(o_done, 2)
            normed(0)
            split_lo(0, 0)
            transposed_lo(0)
            splits("e_cols")
            splits("e_small")

            dve.wait_ge(e_loaded, 16 * 10)
            dve.wait_ge(bank_free, 4 + S["e_small"].unit + 2)
            nc.vector.tensor_tensor(branch_gate[:, :, :], branch_gate[:, :, :],
                                    gate_rows[:, :].unsqueeze(1).broadcast_to([P, NT, NG_COLS]),
                                    ALU.add).then_inc(gates_added, 1)
            dve.wait_ge(e_masks, 1)
            for b_ in range(2):
                dve.wait_ge(gla_pre, b_ + 1)
                chain.link(nc.vector.tensor_scalar(cum[:, b_, :], cum[:, b_, :], 0.0, None, ALU.min))
                chain.link(nc.vector.tensor_tensor(cum[:, b_, :], cum[:, b_, :], t1[:, b_, :], ALU.subtract))
                chain.link(nc.vector.tensor_scalar(cum[:, b_, :], cum[:, b_, :], 1.0 / 16.0, None, ALU.mult))
                chain.link(nc.vector.tensor_tensor_scan(cum[:, b_, :], keep[:, :], cum[:, b_, :], 0.0,
                                                        ALU.mult, ALU.add))
                dve.sem_inc(gla_log, 1)
                c3 = cum[:, b_, :].rearrange("p (n c) -> p n c", c=CH)
                chain.link(nc.vector.tensor_tensor(k_end[:, b_, :].rearrange("p (n c) -> p n c", c=CH),
                                                   c3[:, :, CH - 1:CH].broadcast_to([P, 8, CH]), c3, ALU.subtract))
                dve.sem_inc(gla_log, 1)
            split_next(S["e_v"], 0, 0)
            for b_ in range(2):
                dve.wait_ge(gla_exp, 3 * b_ + 1)
                nc.vector.tensor_tensor(e_t[:, b_, :], e_t[:, b_, :], t1[:, b_, :], ALU.mult).then_inc(gla_ops, 1)
                dve.wait_ge(gla_exp, 3 * b_ + 3)
                chain.link(nc.vector.tensor_tensor(k_end[:, b_, :], k_end[:, b_, :], e_t[:, 2 + b_, :], ALU.mult))
                nc.vector.tensor_tensor(e_t[:, 2 + b_, :], e_t[:, 2 + b_, :], t1[:, b_, :], ALU.mult)\
                    .then_inc(gla_ops, 1)
            split_lo(S["e_v"].first + 2, (S["e_v"].first + 2) % 2)
            split_lo(S["e_v"].first + 3, (S["e_v"].first + 3) % 2)

            dve.wait_ge(bank_free, 4 + 14)
            for step in range(4):
                x, part = divmod(step, 2)
                if step >= 2:
                    dve.wait_ge(cmp_step, step - 1)
                for g in range(2):
                    src = x_c[:, 2 * x + g, :].rearrange("p (c s) -> p s c", s=CMP_STRIDE)
                    o = nc.vector.tensor_tensor(
                        cmp_x[:, step % 2, :, g, :], src[:, 0:CMP_STRIDE:2, part:part + CMP_N],
                        cmp_pos[:, x, 8 * part:8 * part + 8].unsqueeze(2).broadcast_to([P, 8, CMP_N]), ALU.add)
                o.then_inc(cmp_x_ready, 1)

            def keep_causal(v):
                dve.wait_ge(gla_a, v + 1)
                if v >= 2:
                    dve.wait_ge(gla_o, v - 1)
                for j in range(2):
                    o = nc.vector.copy_predicated(am[:, v % 2, j, :], gla_mask[:, :].bitcast(I32),
                                                  ps[:, j, 0:P])
                o.then_inc(gla_am, 1)

            dve.wait_ge(cmp_mm, 1)
            chain.link(nc.vector.memset(state[:, :, 0, :], 0.0))
            keep_causal(0)
            for v in range(8):
                b_, t = divmod(v, 4)
                if v + 1 < 8:
                    keep_causal(v + 1)
                dve.wait_ge(gla_ds, v + 1)
                for c in range(2):
                    n = 2 * t + c
                    if n + 1 < 8:
                        chain.link(nc.vector.scalar_tensor_tensor(
                            state[:, b_, n + 1, :], state[:, b_, n, :], chunk_decay[:, b_, n:n + 1],
                            ps[:, 2 + c, 0:P], ALU.mult, ALU.add))
                dve.sem_inc(gla_s, 1)
            def inverse(hd):
                dve.wait_ge(gn_mm, hd + 1)
                if hd >= 2:
                    dve.wait_ge(gn_rs, hd - 1)
                chain.link(nc.vector.tensor_scalar(gn_inv[:, hd % 2, :], ps[:, 6 + hd % 2, :], 1.0 / P, EPS,
                                                   ALU.mult, ALU.add))
                nc.vector.reciprocal(gn_inv[:, hd % 2, :], gn_inv[:, hd % 2, :]).then_inc(gn_ms, 1)

            inverse(0)
            for hd in range(GLA_HEADS):
                if hd + 1 < GLA_HEADS:
                    inverse(hd + 1)
                dve.wait_ge(gn_rs, hd + 1)
                chain.link(nc.vector.scalar_tensor_tensor(o_gla[:, hd, :], o_gla[:, hd, :], gla_norm[:, hd:hd + 1],
                                                          t1[:, hd % 2, :], ALU.mult, ALU.mult))
                dve.sem_inc(gn_done, 1)
                chain.link(nc.vector.tensor_tensor(o_gla[:, hd, :], o_gla[:, hd, :], e_t[:, 4 + hd, :], ALU.mult))
                chain.link(nc.vector.tensor_copy(mix_hi[:, hd, :], o_gla[:, hd, :]))
                chain.link(nc.vector.tensor_tensor(mix_lo[:, hd, :], o_gla[:, hd, :],
                                                   mix_hi[:, hd, :].bitcast(F32), ALU.subtract))

            def maxes_nsa(su, half, t, it):
                s, nk = su % 2, P * (t + 1)
                st_ = att_stat[:, s, :]
                c = small_scores(s, CMP_N)
                nc.vector.tensor_tensor(c, c, cmp_add[:, t, 0:CMP_N], ALU.add)
                for b_ in range(2):
                    d = ps[:, 2 * s + b_, P * t:P * t + P]
                    o = nc.vector.tensor_tensor(d, d, causal[:, :], ALU.add)
                chain.link(o)
                nc.vector.tensor_reduce(st_[:, 0:1], c, AX.X, ALU.max)
                nc.vector.tensor_reduce(st_[:, 1:2], ps[:, 2 * s, 0:nk], AX.X, ALU.max)
                chain.link(nc.vector.tensor_reduce(st_[:, 2:3], ps[:, 2 * s + 1, 0:nk], AX.X, ALU.max))
                return nc.vector.tensor_scalar(st_[:, 3:6], st_[:, 0:3], -1.0, None, ALU.mult)

            def scale_nsa(su, half, t, it):
                s, nk = su % 2, P * (t + 1)
                st_ = att_stat[:, s, :]
                pc = prob_n[:, s, 0:CMP_N]
                chain.link(nc.vector.tensor_tensor(pc, pc, cmp_one[:, t, 0:CMP_N], ALU.mult))
                chain.link(nc.vector.tensor_reduce(st_[:, 6:7], pc, AX.X, ALU.add))
                chain.link(nc.vector.tensor_scalar(st_[:, 6:9], st_[:, 6:9], 1e-30, None, ALU.max))
                chain.link(nc.vector.reciprocal(st_[:, 9:12], st_[:, 6:9]))
                gate = branch_gate[:, t, bass.ds(it * 6 + 3 * half, 3)]
                chain.link(nc.vector.tensor_tensor(st_[:, 9:12], st_[:, 9:12], gate, ALU.mult))
                nc.vector.tensor_scalar(pc, pc, st_[:, 9:10], None, ALU.mult)
                for b_ in range(2):
                    seg = prob_n[:, s, P + b_ * nk:P + (b_ + 1) * nk]
                    o = nc.vector.tensor_scalar(seg, seg, st_[:, 10 + b_:11 + b_], None, ALU.mult)
                return o

            def maxes_dil(su, half, t, it):
                s, nk, n0 = su % 2, P * (t + 1), P * min(2, t + 1)
                st_ = att_stat[:, s, :]
                slot = it * 2 + half
                segs = [(small_scores(s, n0).unsqueeze(1),
                         bias_near[:, bass.ds(slot, 1), 256 - n0:256])]
                for g in range(2):
                    segs.append((ps[:, 2 * s + g:2 * s + g + 1, 0:nk],
                                 bias_far[:, g, bass.ds(slot, 1), SEQ - nk:SEQ]))
                for seg, bias in segs:
                    o = nc.vector.tensor_tensor(seg, seg, bias, ALU.add)
                chain.link(o)
                nc.vector.tensor_reduce(st_[:, 0:1], small_scores(s, n0), AX.X, ALU.max)
                nc.vector.tensor_reduce(st_[:, 1:2], ps[:, 2 * s, 0:nk], AX.X, ALU.max)
                chain.link(nc.vector.tensor_reduce(st_[:, 2:3], ps[:, 2 * s + 1, 0:nk], AX.X, ALU.max))
                chain.link(nc.vector.tensor_reduce(st_[:, 3:4], st_[:, 0:3], AX.X, ALU.max))
                return nc.vector.tensor_scalar(st_[:, 4:5], st_[:, 3:4], -1.0, None, ALU.mult)

            def scale_dil(su, half, t, it):
                s, n = su % 2, P * dil_tiles(t)
                st_ = att_stat[:, s, :]
                chain.link(nc.vector.tensor_reduce(st_[:, 10:11], st_[:, 7:10], AX.X, ALU.add))
                chain.link(nc.vector.reciprocal(st_[:, 11:12], st_[:, 10:11]))
                return nc.vector.tensor_scalar(prob[:, s, 0:n], prob[:, s, 0:n], st_[:, 11:12], None, ALU.mult)

            def maxes_fox(su, half, t, it):
                s, nk = su % 2, P * (t + 1)
                st_ = att_stat[:, s, :]
                d = ps[:, 2 * s, P * t:P * t + P]
                chain.link(nc.vector.tensor_tensor(d, d, causal[:, :], ALU.add))
                chain.link(nc.vector.tensor_reduce(st_[:, 3:4], ps[:, 2 * s, 0:nk], AX.X, ALU.max))
                return nc.vector.tensor_scalar(st_[:, 4:5], st_[:, 3:4], -1.0, None, ALU.mult)

            def scale_fox(su, half, t, it):
                s, nk = su % 2, P * (t + 1)
                st_ = att_stat[:, s, :]
                chain.link(nc.vector.reciprocal(st_[:, 11:12], st_[:, 7:8]))
                return nc.vector.tensor_scalar(prob[:, s, 0:nk], prob[:, s, 0:nk], st_[:, 11:12], None, ALU.mult)

            def attention(kind, maxes, scale, hi, lo, first_block, links):
                order_ = list(kind.turns())

                def max_unit(su, it):
                    turn, k = (it + 1, 0) if su == kind.units else (it, su)
                    half, t, g0 = order_[k]
                    dve.wait_ge(sc_done, it * kind.units + (kind.unit + su + 1))
                    maxes(k, half, t, turn).then_inc(mx_done, 1)

                def scale_unit(su, it):
                    turn, k = (it + 1, 0) if su == kind.units else (it, su)
                    half, t, g0 = order_[k]
                    dve.wait_ge(ex_done, it * kind.units + (kind.unit + su + 3))
                    scale(k, half, t, turn).then_inc(pr_done, 1)

                def take_out(su, it):
                    half, t, g0 = order_[su]
                    dve.wait_ge(pv_done, it * kind.units + (kind.unit + su + 1))
                    rows_ = slice(half * HD, (half + 1) * HD)
                    src = out_bank(half).unsqueeze(1)
                    blk = bass.ds(it + first_block, 1)
                    chain.link(nc.vector.tensor_copy(hi[rows_, blk, t * P:(t + 1) * P], src))
                    nc.vector.tensor_tensor(lo[rows_, blk, t * P:(t + 1) * P], src,
                                            hi[rows_, blk, t * P:(t + 1) * P].bitcast(F32),
                                            ALU.subtract).then_inc(o_done, 1)

                def body(it):
                    for su in range(kind.units):
                        if not (is_last(kind, it) and su == kind.units - 1):
                            max_unit(su + 1, it)
                            scale_unit(su + 1, it)
                        take_out(su, it)

                max_unit(0, 0)
                scale_unit(0, 0)
                with dve.Fori(0, kind.loops - 1) as it:
                    chain.enter(it, links)
                    body(it)
                chain.leave(kind.loops - 1)
                body(kind.loops - 1)

            attention(nsa, maxes_nsa, scale_nsa, mix_hi, mix_lo, 4, 8 * (2 + 5 + 1))
            splits("e_out")
            post(0, 4, False, 1)

            def two_parts(hi, lo, src):
                chain.link(nc.vector.tensor_copy(hi, src))
                return nc.vector.tensor_tensor(lo, src, hi.bitcast(F32), ALU.subtract)

            def mlp_up(l, part):
                st = S[f"f{l}_up{part}"]

                def turn(i, q, it):
                    split_next(st, i, q)
                    for f in range(2):
                        taken(st, i, f)
                        blk = bass.ds(i * 2 + f, 1)
                        r = work[:, f:f + 1, :]
                        chain.link(nc.vector.tensor_tensor(r, r, r, ALU.mult))
                        two_parts(h2_hi[:, blk, :], h2_lo[:, blk, :], r).then_inc(h2_ready, 1)

                def tiles_chained():
                    pairs = st.count // 2
                    with dve.Fori(0, pairs) as it:
                        chain.enter(it, 8)
                        turn(it * 2, 0, it)
                        turn(it * 2 + 1, 1, it)
                    chain.leave(pairs)
                tiles_chained()

            def ada_take(cc):
                dve.wait_ge(ada_mm, cc + 1)
                if cc in (2, 5):
                    row_ = g1_row if cc == 2 else g2_row
                    nc.vector.tensor_tensor(row_[:, :], row_[:, :], bank_pair(3), ALU.add).then_inc(ada_mod, 1)
                    return
                j = {0: 0, 1: 1, 3: 2, 4: 3}[cc]
                chain.link(nc.vector.tensor_tensor(col_mod[:, j, :], ps[:, 6, 0:DK], b_ada_col[:, DK * cc:DK * cc + DK],
                                                   ALU.add))
                if j % 2 == 0:
                    nc.vector.tensor_copy(col_bias[:, j // 2, :], col_mod[:, j, :]).then_inc(ada_mod, 1)
                else:
                    p = 4 + j // 2
                    nc.vector.scalar_tensor_tensor(col_gain[:, p, :], col_mod[:, j, :], 1.0, col_gain[:, p, :],
                                                   ALU.add, ALU.mult).then_inc(ada_mod, 1)

            def mlp_layer(l, first_pass, e):
                transposed_lo(1 if l == 0 else 3)
                mlp_up(l, 0)
                if l == 0:
                    ada_take(0)
                else:
                    ada_take(5)
                splits(f"f{l}_down0")
                if l == 0:
                    ada_take(1)
                mlp_up(l, 1)
                if l == 0:
                    ada_take(2)
                splits(f"f{l}_down1")
                add_sum(first_pass + 1, True)
                if l == 0:
                    ada_take(3)
                mlp_up(l, 2)
                if l == 0:
                    ada_take(4)
                splits(f"f{l}_down2")
                post(first_pass + 2, e, True, {0: 2, 1: 4}[l])

            mlp_layer(0, 1, 12)

            transposed_lo(2)
            splits("o_u")
            splits("o_v")
            for t in range(NT):
                dve.wait_ge(bank_free, 4 + S["o_v"].unit + 16)
                for c in range(4):
                    o = nc.vector.bn_stats(bn[:, c, :], v_ln[:, t, c * 512:(c + 1) * 512])
                chain.link(o)
                chain.link(nc.vector.bn_aggr(mv[:, t, :], bn[:, :, :]))
                dve.sem_inc(ln_stat, 1)
            for t in range(NT):
                dve.wait_ge(ln_rstd, t + 1)
                nc.vector.tensor_scalar(v_ln[:, t, :], v_ln[:, t, :], mv[:, t, 0:1], mv[:, t, 1:2],
                                        ALU.subtract, ALU.mult).then_inc(ln_done, 1)
            dve.wait_ge(ws_copied, 4)

            def y_part(f):
                dve.wait_ge(y_hi_ready, f + 1)
                nc.vector.tensor_tensor(y_lo[:, f, :], work[:, f % 2, :], y_hi[:, f, :].bitcast(F32),
                                        ALU.subtract).then_inc(y_ready, 1)
            for f in range(16):
                if f >= 2:
                    y_part(f - 2)
                r = small_row[:, :]
                chain.link(nc.vector.scalar_tensor_tensor(r, w_sum[:, f // 2, :], ln_b_col[:, f:f + 1],
                                                          b_s_row[:, f // 2, :], ALU.mult, ALU.add))
                dve.wait_ge(mix_mm, f + 1)
                if f >= 2:
                    dve.wait_ge(y_ready, f - 1)
                w4 = work[:, f % 2, :].rearrange("p (n c) -> p n c", c=P)
                nc.vector.scalar_tensor_tensor(w4, ps[:, f % 4, :].rearrange("p (n c) -> p n c", c=P),
                                               ln_g_col[:, f:f + 1], r.unsqueeze(1).broadcast_to([P, NT, P]),
                                               ALU.mult, ALU.add).then_inc(mix_evac, 1)
                dve.wait_ge(mix_evac, f + 1)
                nc.vector.tensor_tensor(work[:, f % 2, :], work[:, f % 2, :], u_t[:, f, :], ALU.mult)\
                    .then_inc(y_value, 1)
            y_part(14)
            y_part(15)
            splits("o_out")
            post(4, 20, False, 3)

            mlp_layer(1, 5, 28)

            transposed_lo(4)
            splits("s_qk")
            dve.wait_ge(f_made, 1)
            chain.link(nc.vector.tensor_copy(dist[:, :], dist_i[:, :]))
            for g, (_, dilation) in enumerate(DILATED):
                neg_i = far_neg[:, g, :].bitcast(I32)
                chain.link(nc.vector.tensor_scalar(neg_i, dist_i[:, :], dilation - 1, None, ALU.bitwise_and))
                chain.link(nc.vector.tensor_copy(far_neg[:, g, :], neg_i))
                chain.link(nc.vector.tensor_scalar(far_neg[:, g, :], far_neg[:, g, :], 1.0, NEG, ALU.min, ALU.mult))
            dve.sem_inc(f_made, 1)
            dve.wait_ge(f_made, 3)
            for g in range(3):
                for slot in range(SLOTS):
                    slope = -ALIBI[g * SLOTS + slot]
                    if g == 0:
                        o = nc.vector.scalar_tensor_tensor(bias_near[:, slot, :], dist[:, 256:SEQ], slope,
                                                           far_neg[:, 0, 256:SEQ], ALU.mult, ALU.add)
                    else:
                        o = nc.vector.scalar_tensor_tensor(bias_far[:, g - 1, slot, :], dist[:, :], slope,
                                                           far_neg[:, g, :], ALU.mult, ALU.add)
            chain.link(o)
            splits("s_v")
            splits("s_small")
            dve.wait_ge(f_sum, 1)
            fa, fb, fc = f_row[0:4, :], prob[0:4, 0, 0:SEQ], prob[0:4, 1, 0:SEQ]
            chain.link(nc.vector.memset(fc, 1.0))
            chain.link(nc.vector.tensor_scalar(fa, fa, 0.0, None, ALU.min))
            chain.link(nc.vector.tensor_tensor(fb, fb, fa, ALU.subtract))
            chain.link(nc.vector.tensor_tensor_scan(fa, fc, fb, 0.0, ALU.mult, ALU.add))
            dve.sem_inc(f_made, 1)
            attention(dil, maxes_dil, scale_dil, yt_hi, yt_lo, 0, 8 * (3 + 2 + 1))
            attention(fox, maxes_fox, scale_fox, yt_hi, yt_lo, 2, 8 * (2 + 1 + 1))
            splits("s_upa")
            splits("s_upb")
            for name, up in (("s_ga", up_a), ("s_gb", up_b)):
                st = S[name]
                links = 0 if name == "s_ga" else 4 * 3
                with dve.Fori(0, 2) as it:
                    chain.enter(it, links)
                    for q in range(2):
                        i = it * 2 + q
                        split_next(st, i, q)
                        for f in range(2):
                            taken(st, i, f)
                            blk = bass.ds(i * 2 + f, 1)
                            mul = nc.vector.tensor_tensor(up[:, blk, :], up[:, blk, :], work[:, f:f + 1, :], ALU.mult)
                            if name == "s_ga":
                                mul.then_inc(gate_used, 1)
                            else:
                                chain.link(mul)
                                chain.link(nc.vector.tensor_tensor(up_a[:, blk, :], up_a[:, blk, :],
                                                                   up_b[:, blk, :], ALU.add))
                                two_parts(mg_hi[:, blk, :], mg_lo[:, blk, :], up_a[:, blk, :])\
                                    .then_inc(gate_used, 1)
                chain.leave(2)
            splits("s_out")
            for t in range(NT):
                dve.wait_ge(mm_done, sum_done(8, t))
                chain.link(nc.vector.tensor_tensor(m[:, t, :], bank_pair(t), g1_row[:, :], ALU.mult))
                nc.vector.tensor_tensor(h[:, t, :], h[:, t, :], m[:, t, :], ALU.add).then_inc(h_ready, 1)
            normed(36)

            transposed_lo(5)
            for part in range(2):
                st = S[f"g_up{part}"]
                with dve.Fori(0, st.count // 2) as it:
                    chain.enter(it, 2)
                    for q in range(2):
                        i = it * 2 + q
                        split_next(st, i, q)
                        if q == 0:
                            continue
                        for f in range(2):
                            blk, w_ = bass.ds(it * 2 + f, 1), work[:, f:f + 1, :]
                            taken(st, it * 2, f)
                            dve.wait_ge(mm_done, it * 4 + (st.done + 2 + f + 1))
                            nc.vector.tensor_tensor(w_, w_, ps[:, (st.unit + 2 + f) % 4, :].unsqueeze(1),
                                                    ALU.mult).then_inc(up_ready, 1)
                            dve.wait_ge(up_ready, it * 2 + (12 * part + f + 1))
                            two_parts(h2_hi[:, blk, :], h2_lo[:, blk, :], w_).then_inc(h2_ready, 1)
                chain.leave(st.count // 2)
                splits(f"g_down{part}")
            dve.wait_ge(rows_loaded, 16 * 5)
            for t in range(NT):
                dve.wait_ge(mm_done, sum_done(10, t))
                chain.link(nc.vector.tensor_tensor(m[:, t, :], m[:, t, :], bank_pair(t), ALU.add))
                chain.link(nc.vector.tensor_tensor(m[:, t, :], m[:, t, :], g2_row[:, :], ALU.mult))
                nc.vector.tensor_tensor(h[:, t, :], h[:, t, :], m[:, t, :], ALU.add).then_inc(h_ready, 1)
            for t in range(NT):
                c = (40 + t) % 16
                dve.wait_ge(rstd_ready, 40 + t + 1)
                nc.vector.scalar_tensor_tensor(m[:, t, :], h[:, t, :], rstd[:, c:c + 1], row_gain[:, :],
                                               ALU.mult, ALU.mult).then_inc(final_done, 1)

        @block.tensor
        def _(pe):
            def mm3(dst, a_hi, a_lo, b_hi, b_lo, start, stop_):
                nc.tensor.matmul(dst, a_hi, b_hi, start=start, stop=False)
                nc.tensor.matmul(dst, a_hi, b_lo, start=False, stop=False)
                return nc.tensor.matmul(dst, a_lo, b_hi, start=False, stop=stop_)

            def transposes(p, first_square):
                for t in range(NT):
                    pe.wait_ge(xs_ready, 4 * p + t + 1)
                    for k in range(DK):
                        o = nc.tensor.transpose(ps[:, k, t * P:(t + 1) * P], m[:, t, k * P:(k + 1) * P], ident[:, :])
                        if t == NT - 1:
                            o.then_inc(xt_done, 1)

            def turned(name, body=None):
                st = S[name]

                def turn(i, q, it):
                    s = (st.first + q) % 2
                    pe.wait_ge(w_lo_ready, i + (st.first + 1))
                    hi, lo = by8(w_hi, s), by8(w_lo, s)
                    for f in range(2):
                        b_ = (st.unit + 2 * q + f) % 4
                        pe.wait_ge(bank_free, i * 2 + (st.unit + f + 1))
                        cols = slice(f * P, (f + 1) * P)
                        for k in range(DK):
                            o = mm3(ps[:, b_, :], hi[:, k, cols], lo[:, k, cols], x_hi[:, k, :], x_lo[:, k, :],
                                    k == 0, k == DK - 1)
                        o.then_inc(mm_done, 1)
                tiles(pe, st, turn)

            def straight(name):
                st = S[name]

                def turn(i, q, it):
                    s = (st.first + q) % 2
                    pe.wait_ge(w_lo_ready, i + (st.first + 1))
                    hi, lo = by8(w_hi, s), by8(w_lo, s)
                    for t in range(NT):
                        b_ = (st.unit + 2 * q + t // 2) % 4
                        if t % 2 == 0:
                            pe.wait_ge(bank_free, i * 2 + (st.unit + t // 2 + 1))
                        for k in range(DK):
                            toks = slice(t * P, (t + 1) * P)
                            o = mm3(ps[:, b_, (t % 2) * 256:(t % 2) * 256 + 256], x_hi[:, k, toks], x_lo[:, k, toks],
                                    hi[:, k, :], lo[:, k, :], k == 0, k == DK - 1)
                        if t % 2:
                            o.then_inc(mm_done, 1)
                tiles(pe, st, turn)

            def summed(name, pass_no, a_hi, a_lo, ready=None, base=0):
                st = S[name]

                def turn(i, s, first, last_):
                    pe.wait_ge(w_lo_ready, i + (st.first + 1))
                    if ready is not None:
                        pe.wait_ge(ready, i * 2 + (base + 2))
                    hi, lo = by2(w_hi, s), by2(w_lo, s)
                    for t in range(NT):
                        for half in range(2):
                            for kk in range(2):
                                k = i * 2 + kk
                                toks = slice(t * P, (t + 1) * P)
                                cols = slice(half * 512, half * 512 + 512)
                                o = mm3(ps[:, 2 * t + half, :], a_hi[:, k, toks], a_lo[:, k, toks], hi[:, kk, cols], lo[:, kk, cols],
                                        first and kk == 0, last_ and kk == 1)
                        if last_ or t == NT - 1:
                            o.then_inc(mm_done, 1)

                for i in range(st.count):
                    turn(i, (st.first + i) % 2, i == 0, i == st.count - 1)

            def all_units(name):
                st = S[name]
                per = 2
                pe.wait_ge(bank_free, 4 + st.unit + st.count * per)

            pe.wait_ge(consts_made, 1)
            transposes(0, 0)
            pe.wait_ge(x_ready, DK)
            turned("e_cols")
            st = S["e_small"]
            s = st.first % 2
            pe.wait_ge(w_lo_ready, st.first + 1)
            pe.wait_ge(bank_free, st.unit + 1)
            hi, lo = by8(w_hi, s), by8(w_lo, s)
            for k in range(DK):
                o = mm3(ps[:, st.unit % 4, :], hi[:, k, 0:P], lo[:, k, 0:P], x_hi[:, k, :], x_lo[:, k, :],
                        k == 0, k == DK - 1)
            o.then_inc(mm_done, 1)
            pe.wait_ge(bank_free, st.unit + 2)
            for t in range(NT):
                toks = slice(t * P, (t + 1) * P)
                for k in range(DK):
                    o = mm3(ps[:, (st.unit + 1) % 4, t * NG_COLS:(t + 1) * NG_COLS], x_hi[:, k, toks],
                            x_lo[:, k, toks], hi[:, k, P:P + NG_COLS], lo[:, k, P:P + NG_COLS], k == 0, k == DK - 1)
            o.then_inc(mm_done, 1)

            pe.wait_ge(e_loaded, 16 * 10)
            pe.wait_ge(bank_free, 4 + st.unit + 1)
            for b_ in range(2):
                nc.tensor.matmul(ps[:, 6 + b_, :], w_gate[0:RANK, b_ * P:(b_ + 1) * P], f_row[0:RANK, :],
                                 start=True, stop=True).then_inc(gla_mm, 1)
            straight("e_v")

            pe.wait_ge(cmp_loaded, 32)
            for step in range(4):
                x, part = divmod(step, 2)
                pe.wait_ge(cmp_x_ready, step + 1)
                for a in range(8):
                    o = nc.tensor.matmul(ps[:, 4, 2 * CMP_N * x:2 * CMP_N * (x + 1)], cmp_w1[x][:, 8 * part + a, :],
                                         cmp_x[:, step % 2, a, :, :].rearrange("p g c -> p (g c)"),
                                         start=(part == 0 and a == 0), stop=(part == 1 and a == 7))
                o.then_inc(cmp_step if step < 3 else cmp_mm, 1)
            pe.wait_ge(cmp_act, 1)
            for g in range(2):
                for half in range(2):
                    nc.tensor.matmul(ps[half * HD:(half + 1) * HD, 5, 32 * g:32 * g + CMP_N], cmp_w2[:, 0, :],
                                     cmp_hid[:, g, 0:CMP_N], start=True, stop=True)
            for g in range(2):
                o = nc.tensor.matmul(ps[0:CMP_N, 5, 64 + HD * g:64 + HD * (g + 1)], cmp_hid[:, 2 + g, 0:CMP_N],
                                     cmp_w2[:, 1, :], start=True, stop=True)
            o.then_inc(cmp_mm, 1)
            pe.wait_ge(cmp_act, 2)

            pe.wait_ge(bank_free, 4 + S["e_v"].unit + 6)

            def scores_gla(v):
                b_, t = divmod(v, 4)
                toks = slice(t * P, (t + 1) * P)
                if t == 0:
                    pe.wait_ge(gla_ops, 2 * b_ + 2)
                if v:
                    pe.wait_ge(gla_am, v)
                if v >= 2:
                    pe.wait_ge(gla_ket, v - 1)
                for j in range(2):
                    r = slice(j * HD, (j + 1) * HD)
                    nc.tensor.matmul(ps[:, j, 0:P], e_t[r, 2 + b_, toks], e_t[r, b_, toks],
                                     start=True, stop=True)
                nc.tensor.transpose(ps[:, 6 + v % 2, 0:P], k_end[:, b_, toks], ident[:, :]).then_inc(gla_a, 1)

            scores_gla(0)
            for v in range(8):
                b_, t = divmod(v, 4)
                if v + 1 < 8:
                    scores_gla(v + 1)
                pe.wait_ge(gla_ket, v + 1)
                if v:
                    pe.wait_ge(gla_s, v)
                for c in range(2):
                    r = slice(c * CH, (c + 1) * CH)
                    for j in range(2):
                        hd = 2 * b_ + j
                        o = nc.tensor.matmul(ps[j * HD:(j + 1) * HD, 2 + c, 0:P],
                                             k_end_t[r, v % 2, j * HD:(j + 1) * HD], g_v[r, t, hd * P:(hd + 1) * P],
                                             start=True, stop=True)
                o.then_inc(gla_ds, 1)
                pe.wait_ge(gla_am, v + 1)
                pe.wait_ge(gla_s, v + 1)
                if v:
                    pe.wait_ge(gla_oe, v)
                for j in range(2):
                    hd = 2 * b_ + j
                    r = slice(j * HD, (j + 1) * HD)
                    for c in range(2):
                        cols = slice(c * CH, (c + 1) * CH)
                        nc.tensor.matmul(ps[:, 4 + j, cols], g_v[:, t, hd * P:(hd + 1) * P], am[:, v % 2, j, cols],
                                         start=True, stop=False)
                        o = nc.tensor.matmul(ps[:, 4 + j, cols], state[r, b_, 2 * t + c, :],
                                             e_t[r, b_, t * P + c * CH:t * P + (c + 1) * CH],
                                             start=False, stop=True)
                o.then_inc(gla_o, 1)
            for hd in range(GLA_HEADS):
                pe.wait_ge(gn_sq, hd + 1)
                if hd >= 2:
                    pe.wait_ge(gn_ms, hd - 1)
                sq = cum[:, hd % 2, :] if hd < 2 else state_flat[:, hd % 2, :]
                nc.tensor.matmul(ps[:, 6 + hd % 2, :], ones[:, :], sq, start=True,
                                 stop=True).then_inc(gn_mm, 1)

            def scores_nsa(s, half, t, it, first):
                g, nk = it // 2, P * (t + 1)
                r = slice(half * HD, (half + 1) * HD)
                q = e_t[r, bass.ds(it + 8, 1), t * P:(t + 1) * P].rearrange("p o c -> p (o c)")
                if first:
                    return nc.tensor.matmul(small_scores(s, CMP_N), q, k_cmp[r, g, 0:CMP_N], start=True, stop=True)
                nc.tensor.matmul(ps[:, 2 * s, 0:nk], q, k_s[r, g, 0:nk], start=True, stop=True)
                return nc.tensor.matmul(ps[:, 2 * s + 1, 0:nk], q, k_w[r, g, 0:nk], start=True, stop=True)

            def values_nsa(half, t, it, i):
                g = it // 2
                if i == 0:
                    return v_cmp[:, g, :]
                kt = (i - 1) % (t + 1)
                first = P if i - 1 > t else 0
                return v_sw[:, kt, first + g * HD:first + (g + 1) * HD]

            def scores_dil(s, half, t, it, first):
                nk, n0 = P * (t + 1), P * min(2, t + 1)
                r = slice(half * HD, (half + 1) * HD)

                def blk(j):
                    return bass.ds(it + j, 1)

                def q(j):
                    return q_k[r, blk(j), t * P:(t + 1) * P].rearrange("p o c -> p (o c)")
                if first:
                    return nc.tensor.matmul(small_scores(s, n0), q(0),
                                            q_k[r, blk(6), nk - n0:nk].rearrange("p o c -> p (o c)"),
                                            start=True, stop=True)
                for j in range(2):
                    o = nc.tensor.matmul(ps[:, 2 * s + j, 0:nk], q(2 + 2 * j),
                                         q_k[r, blk(8 + 2 * j), 0:nk].rearrange("p o c -> p (o c)"),
                                         start=True, stop=True)
                return o

            def values_dil(half, t, it, i):
                n0 = min(2, t + 1)
                if i < n0:
                    kt, first = t + 1 - n0 + i, 0
                else:
                    kt, first = (i - n0) % (t + 1), 256 * (1 + (i - n0) // (t + 1))
                return v_ab[:, kt, bass.ds(it * P + (first + half * HD), HD)]

            def scores_fox(s, half, t, it, first):
                nk = P * (t + 1)
                r = slice(half * HD, (half + 1) * HD)
                q = q_k[r, bass.ds(it + 12, 1), t * P:(t + 1) * P].rearrange("p o c -> p (o c)")
                k = q_k[r, bass.ds(it + 14, 1), 0:nk].rearrange("p o c -> p (o c)")
                nc.tensor.matmul(ps[:, 2 * s, 0:nk], q, k, start=True, stop=False)
                sel = ident[0:4, bass.ds(it * 2 + half, 1)].broadcast_to([4, P])
                return nc.tensor.matmul(ps[:, 2 * s, 0:nk], sel, f_row[0:4, 0:nk], start=False, stop=True)

            def values_fox(half, t, it, i):
                return v_ab[:, i, bass.ds(it * P + (768 + half * HD), HD)]

            def attention(kind, scores, values, probs):
                order_ = [(it, half, t, it * kind.groups + (kind.group + g0))
                          for it in range(kind.loops) for half, t, g0 in kind.turns()]

                def long_scores(u):
                    it, half, t, g0 = order_[u]
                    pe.wait_ge(ex_done, kind.unit + u + 1)
                    o = scores(u % 2, half, t, it, False)
                    if kind is fox:
                        o.then_inc(sc_done, 1)

                def short_scores(u):
                    if kind is not fox:
                        it, half, t, g0 = order_[u]
                        pe.wait_ge(ex_done, kind.unit + u + 2)
                        scores(u % 2, half, t, it, True).then_inc(sc_done, 1)

                for u in range(2):
                    long_scores(u)
                    short_scores(u)
                for u, (it, half, t, g0) in enumerate(order_):
                    n, s = kind.key_tiles(t), u % 2
                    pe.wait_ge(pr_done, kind.unit + u + 1)

                    def turn_group(gr):
                        pe.wait_ge(pt_done, g0 + gr + 1)
                        for i in range(4 * gr, min(n, 4 * gr + 4)):
                            o = nc.tensor.transpose(ps[:, 5 + (g0 + gr) % 2, (i - 4 * gr) * P:(i - 4 * gr + 1) * P],
                                                    probs[:, s, i * P:(i + 1) * P], ident[:, :])
                        o.then_inc(tr_done, 1)

                    def value_group(gr):
                        pe.wait_ge(pt_done, g0 + gr + 3)
                        if gr == 0:
                            pe.wait_ge(o_done, kind.unit + u + 2)
                        for i in range(4 * gr, min(n, 4 * gr + 4)):
                            o = nc.tensor.matmul(out_bank(half), values(half, t, it, i),
                                                 prob_t[:, (g0 + gr) % 2, (i - 4 * gr) * P:(i - 4 * gr + 1) * P],
                                                 start=(i == 0), stop=(i == n - 1))
                        if gr == groups(n) - 1:
                            o.then_inc(pv_done, 1)

                    turn_group(0)
                    for gr in range(groups(n)):
                        if gr + 1 < groups(n):
                            turn_group(gr + 1)
                        elif u + 2 < len(order_):
                            long_scores(u + 2)
                        value_group(gr)
                    if u + 2 < len(order_):
                        short_scores(u + 2)

            pe.wait_ge(gn_ms, 4)
            pe.wait_ge(gla_oe, 8)
            attention(nsa, scores_nsa, values_nsa, prob_n)
            pe.wait_ge(o_done, 2 + 32)
            summed("e_out", 0, mix_hi, mix_lo)

            def ada(cc):
                pe.wait_ge(ada_sum, cc + 1)
                if cc in (2, 5):
                    for half in range(2):
                        o = nc.tensor.matmul(ps[:, 6 + half, :], ones[:, :], ada_acc[:, half * 512:(half + 1) * 512],
                                             start=True, stop=True)
                else:
                    for k in range(DK):
                        o = nc.tensor.matmul(ps[:, 6, k:k + 1], ada_acc[:, k * P:(k + 1) * P], ones[:, 0:1],
                                             start=True, stop=True)
                o.then_inc(ada_mm, 1)

            def mlp_layer(l, first_pass, frees):
                pe.wait_ge(x_ready, DK * ((1 if l == 0 else 3) + 1))
                turned(f"f{l}_up0")
                ada(0 if l == 0 else 5)
                pe.wait_ge(ada_mod, 1 if l == 0 else 6)
                all_units(f"f{l}_up0")
                summed(f"f{l}_down0", first_pass, h2_hi, h2_lo, h2_ready, 2 + h2_base(f"f{l}_0"))
                pe.wait_ge(acc_free, frees + 4)
                if l == 0:
                    ada(1)
                turned(f"f{l}_up1")
                if l == 0:
                    pe.wait_ge(ada_mod, 2)
                    ada(2)
                    pe.wait_ge(ada_mod, 3)
                all_units(f"f{l}_up1")
                summed(f"f{l}_down1", first_pass + 1, h2_hi, h2_lo, h2_ready, 2 + h2_base(f"f{l}_1"))
                pe.wait_ge(acc_free, frees + 8)
                if l == 0:
                    ada(3)
                turned(f"f{l}_up2")
                if l == 0:
                    pe.wait_ge(ada_mod, 4)
                    ada(4)
                    pe.wait_ge(ada_mod, 5)
                all_units(f"f{l}_up2")
                summed(f"f{l}_down2", first_pass + 2, h2_hi, h2_lo, h2_ready, 2 + h2_base(f"f{l}_2"))

            pe.wait_ge(squares, 8)
            transposes(1, 0)
            mlp_layer(0, 1, 0)
            pe.wait_ge(squares, 16)
            transposes(2, 0)
            pe.wait_ge(x_ready, DK * 3)
            pe.wait_ge(s_masks, 1)
            for g in range(8):
                o = nc.tensor.transpose(ps[:, 4 + g // 4, (g % 4) * P:(g % 4 + 1) * P], w_s[:, g, :], ident[:, :])
                if g % 4 == 3:
                    o.then_inc(ws_mm, 1)
            for half in range(2):
                pe.wait_ge(ws_copied, half + 1)
                nc.tensor.matmul(ps[:, 6 + half, :], ones[:, :],
                                 w_st[:, 4 * half:4 * half + 4, :].rearrange("p g t -> p (g t)"),
                                 start=True, stop=True).then_inc(ws_mm, 1)
            turned("o_u")
            straight("o_v")
            pe.wait_ge(ln_done, 4)
            pe.wait_ge(bank_free, 4 + S["o_v"].unit + 16)
            for f in range(16):
                if f >= 4:
                    pe.wait_ge(mix_evac, f - 3)
                for t in range(NT):
                    o = nc.tensor.matmul(ps[:, f % 4, t * P:(t + 1) * P], v_ln[:, t, f * P:(f + 1) * P],
                                         w_st[:, f // 2, :], start=True, stop=True)
                o.then_inc(mix_mm, 1)
            pe.wait_ge(mix_evac, 16)
            pe.wait_ge(ws_copied, 4)
            summed("o_out", 4, y_hi, y_lo, y_ready, 0)
            pe.wait_ge(squares, 24)
            transposes(3, 0)
            mlp_layer(1, 5, 8)
            pe.wait_ge(squares, 32)
            transposes(4, 0)
            pe.wait_ge(x_ready, DK * 5)
            turned("s_qk")
            straight("s_v")
            st = S["s_small"]
            s = st.first % 2
            pe.wait_ge(w_lo_ready, st.first + 1)
            pe.wait_ge(bank_free, st.unit + 1)
            hi, lo = by8(w_hi, s), by8(w_lo, s)
            for k in range(DK):
                o = mm3(ps[:, st.unit % 4, :], hi[:, k, 0:P], lo[:, k, 0:P], x_hi[:, k, :], x_lo[:, k, :],
                        k == 0, k == DK - 1)
            o.then_inc(mm_done, 1)
            pe.wait_ge(f_sum, 1)
            pe.wait_ge(bank_free, 4 + st.unit + 1)
            attention(dil, scores_dil, values_dil, prob)
            pe.wait_ge(f_made, 4)
            attention(fox, scores_fox, values_fox, prob)
            pe.wait_ge(o_done, 2 + 64)
            for name, first in (("s_upa", 0), ("s_upb", 2)):
                st = S[name]
                s = st.first % 2
                pe.wait_ge(w_lo_ready, st.first + 1)
                hi, lo = by2(w_hi, s), by2(w_lo, s)
                for f in range(DK):
                    pe.wait_ge(bank_free, st.unit + f + 1)
                    cols = slice(f * P, (f + 1) * P)
                    for k in range(2):
                        o = mm3(ps[:, (st.unit + f) % 4, :], hi[:, k, cols], lo[:, k, cols],
                                yt_hi[:, first + k, :], yt_lo[:, first + k, :], k == 0, k == 1)
                    o.then_inc(mm_done, 1)
            turned("s_ga")
            turned("s_gb")
            all_units("s_gb")
            summed("s_out", 8, mg_hi, mg_lo, gate_used, 2 + DK)
            pe.wait_ge(h_ready, 20)
            transposes(5, 0)
            pe.wait_ge(x_ready, DK * 6)
            turned("g_up0")
            all_units("g_up0")
            summed("g_down0", 9, h2_hi, h2_lo, h2_ready, 2 + h2_base("g_0"))
            pe.wait_ge(acc_free, 20)
            turned("g_up1")
            all_units("g_up1")
            summed("g_down1", 10, h2_hi, h2_lo, h2_ready, 2 + h2_base("g_1"))


_INS = ['x', 'norm_g', 'ffn_w1', 'ffn_w2', 'e_w_in', 'e_w_out', 'gla_w_gate', 'gla_b_gate', 'gla_norm', 'nsa_gate_b',
        'nsa_cmp_pos', 'nsa_cmp_w1', 'nsa_cmp_w2', 'o_w_in', 'o_ln_g', 'o_ln_b', 'o_w_s', 'o_b_s', 'o_w_out', 'c_2',
        'w_ada_2', 'b_ada_2', 'norm_mix_2', 'w_in_2', 'b_forget_2', 'w_up_a_2', 'w_up_b_2', 'w_out_2', 'norm_ffn_2',
        'w_ffn_in_2', 'w_ffn_out_2', 'norm_final_2']


def kernel(**inputs):
    import concourse.bacc as _bacc
    from concourse.bass_utils import run_bass_kernel_spmd as _run

    nc = _bacc.Bacc("TRN2", target_bir_lowering=False, num_devices=1)
    arrays, views = {}, {}
    for name in _INS:
        a = np.ascontiguousarray(inputs[name])
        arrays[f"in_{name}"] = a
        views[name] = nc.dram_tensor(f"in_{name}", a.shape, mybir.dt.from_np(a.dtype), kind="ExternalInput").ap()
    out = nc.dram_tensor("out_0", (1, SEQ, D), F32, kind="ExternalOutput").ap()
    program(nc, views, out)
    return _run(nc, [arrays], core_ids=[0]).results[0]["out_0"]
```
